# Optimizing a Trainium2 kernel written in Bass

```python
import jax
import jax.numpy as jnp
from jax import lax
import numpy as np

D_MODEL = 1024
BATCH = 1
SEQ = 1024
DEPTH = 2
DEC_BATCH = 8
DEC_SEQ = 4
PAST_LEN = 1024
PAGE_SIZE = 128

N_EVEN = (DEPTH + 1) // 2
N_ODD = DEPTH // 2
A_HEADS = 4
A_HEAD_DIM = D_MODEL // 8
A_WIDTH = A_HEADS * A_HEAD_DIM
A_CHUNK = 128
B_HEADS = 4
B_HEAD_DIM = D_MODEL // 8
B_WIDTH = B_HEADS * B_HEAD_DIM
B_CHUNK = 64
C_HEADS = 16
C_HEAD_DIM = D_MODEL // C_HEADS
C_WIDTH = C_HEADS * C_HEAD_DIM
C_QBLOCK = 128
C_BIAS_INIT = -7.0
FFN_HIDDEN = -(-8 * D_MODEL // (3 * 256)) * 256
DN_ALPHA = (2 * DEPTH) ** 0.25
DN_BETA = (8 * DEPTH) ** -0.25
LN_EPS = 1e-5
RMS_EPS = 1e-6
AB_SPLITS = [A_WIDTH, 2 * A_WIDTH, 2 * A_WIDTH + B_WIDTH, 2 * A_WIDTH + 2 * B_WIDTH, 2 * A_WIDTH + 3 * B_WIDTH]
AB_IN = 2 * A_WIDTH + 4 * B_WIDTH

kernel_name = 'hybrid_gmlp_hgrn2_stickbreak_step'

def layer_norm(x, g, b):
    xf = x.astype(jnp.float32)
    mu = jnp.mean(xf, -1, keepdims=True)
    var = jnp.mean(jnp.square(xf - mu), -1, keepdims=True)
    return ((xf - mu) * lax.rsqrt(var + LN_EPS) * g.astype(jnp.float32) + b.astype(jnp.float32)).astype(x.dtype)

def swiglu(h, wg, wu, wd):
    return (jax.nn.silu(h @ wg) * (h @ wu)) @ wd

def chunk_gmlp(u, v, w_s, b_s, ln_g, ln_b):
    N, L, _ = u.shape
    vh = layer_norm(v.reshape(N, L, A_HEADS, A_HEAD_DIM), ln_g.reshape(A_HEADS, A_HEAD_DIM), ln_b.reshape(A_HEADS, A_HEAD_DIM))
    Lp = -(-L // A_CHUNK) * A_CHUNK
    vc = jnp.pad(vh, ((0, 0), (0, Lp - L), (0, 0), (0, 0))).reshape(N, Lp // A_CHUNK, A_CHUNK, A_HEADS, A_HEAD_DIM)
    w = jnp.where(jnp.tril(jnp.ones((A_CHUNK, A_CHUNK), bool)), w_s, 0)
    sv = jnp.einsum('hts,ncshd->ncthd', w.astype(vc.dtype), vc) + b_s.T[None, None, :, :, None]
    sv = sv.reshape(N, Lp, A_WIDTH)[:, :L]
    return u * sv, vh.reshape(N, L, A_WIDTH)

def hgrn2_chunked(q, k, v, log_f, s0):
    N, L, H, _ = q.shape
    c = min(B_CHUNK, L)
    Lp = -(-L // c) * c
    n_chunks = Lp // c
    pad = ((0, 0), (0, Lp - L), (0, 0), (0, 0))

    def chunks(a):
        a = jnp.pad(a, pad)
        return a.reshape(N, n_chunks, c, H, a.shape[-1]).transpose(1, 0, 3, 2, 4)

    causal = jnp.tril(jnp.ones((c, c), bool))[:, :, None]

    def step(S, inp):
        qc, kc, vc, lf = inp
        G = jnp.cumsum(lf, axis=2)
        o_inter = jnp.einsum('nhtk,nhkv->nhtv', qc * jnp.exp(G), S)
        decay = jnp.exp(jnp.where(causal, G[:, :, :, None, :] - G[:, :, None, :, :], -jnp.inf))
        scores = jnp.einsum('nhtk,nhsk,nhtsk->nhts', qc, kc, decay)
        o_intra = jnp.einsum('nhts,nhsv->nhtv', scores, vc)
        G_last = G[:, :, -1:, :]
        S_new = jnp.exp(G_last[:, :, 0, :])[..., None] * S + jnp.einsum('nhsk,nhsv->nhkv', kc * jnp.exp(G_last - G), vc)
        return S_new, o_inter + o_intra

    S_fin, o = lax.scan(step, s0, (chunks(q), chunks(k), chunks(v), chunks(log_f)))
    o = o.transpose(1, 0, 3, 2, 4).reshape(N, Lp, H, v.shape[-1])[:, :L]
    return o, S_fin

def mixer_ab(h, s0, w_in, w_out, a_w_s, a_b_s, a_ln_g, a_ln_b, lb, b_norm_g):
    N, L, _ = h.shape
    u, v, bq, bf, bi, bg = jnp.split(h @ w_in, AB_SPLITS, axis=-1)
    a_out, a_v = chunk_gmlp(jax.nn.gelu(u), jax.nn.gelu(v), a_w_s, a_b_s, a_ln_g, a_ln_b)
    heads = lambda t: t.astype(jnp.float32).reshape(N, L, B_HEADS, B_HEAD_DIM)
    f_pre = heads(bf)
    lb = lb.reshape(B_HEADS, B_HEAD_DIM)
    log_f = jnp.log(lb + (1.0 - lb) * jax.nn.sigmoid(f_pre))
    k = (1.0 - lb) * jax.nn.sigmoid(-f_pre)
    o, s_new = hgrn2_chunked(jax.nn.silu(heads(bq)), k, heads(bi), log_f, s0.astype(jnp.float32))
    o = o * lax.rsqrt(jnp.mean(o * o, -1, keepdims=True) + RMS_EPS) * b_norm_g.astype(jnp.float32)
    o = (o.reshape(N, L, B_WIDTH) * jax.nn.silu(bg.astype(jnp.float32))).astype(h.dtype)
    y = jnp.concatenate([a_out, o], axis=-1) @ w_out
    return y, a_v, s_new.astype(h.dtype)

def stick_breaking(q, k, v, bias, q_pos, k_pos):
    z = jnp.einsum('nqhd,nkhd->nhqk', q, k).astype(jnp.float32) * (C_HEAD_DIM ** -0.5) + bias.astype(jnp.float32)[None, :, None, None]
    mask = (k_pos[None, :] < q_pos[:, None])[None, None]
    log_beta = jax.nn.log_sigmoid(z)
    log_1m = jnp.where(mask, jax.nn.log_sigmoid(-z), 0.0)
    rest = lax.cumsum(log_1m, axis=3, reverse=True) - log_1m
    w = jnp.where(mask, jnp.exp(log_beta + rest), 0.0)
    return jnp.einsum('nhqk,nkhd->nqhd', w, v.astype(jnp.float32)).astype(q.dtype)

def stick_breaking_blocks(q, k, v, bias, q_pos, k_pos):
    N, Lq, H, dh = q.shape
    qb = min(C_QBLOCK, Lq)
    Lp = -(-Lq // qb) * qb
    nb = Lp // qb
    qblocks = jnp.pad(q, ((0, 0), (0, Lp - Lq), (0, 0), (0, 0))).reshape(N, nb, qb, H, dh).transpose(1, 0, 2, 3, 4)
    pblocks = jnp.pad(q_pos, (0, Lp - Lq), mode='edge').reshape(nb, qb)
    out = lax.map(lambda a: stick_breaking(a[0], k, v, bias, a[1], k_pos), (qblocks, pblocks))
    return out.transpose(1, 0, 2, 3, 4).reshape(N, Lp, H, dh)[:, :Lq]

def qkv_heads(h, w_in):
    N, L, _ = h.shape
    q, k, v = jnp.split(h @ w_in, 3, axis=-1)
    r = lambda t: t.reshape(N, L, C_HEADS, C_HEAD_DIM)
    return r(q), r(k), r(v)

def mixer_c_prompt(h, w_in, w_out, bias):
    N, L, _ = h.shape
    q, k, v = qkv_heads(h, w_in)
    pos = jnp.arange(L, dtype=jnp.int32)
    o = stick_breaking_blocks(q, k, v, bias, pos, pos)
    return o.reshape(N, L, C_WIDTH) @ w_out, k, v

def mixer_c_sample(h, pool_k, pool_v, page_table, w_in, w_out, bias):
    N, L, _ = h.shape
    q, k, v = qkv_heads(h, w_in)
    past = page_table.shape[1] * PAGE_SIZE
    k_past = jnp.take(pool_k, page_table, axis=0).reshape(N, past, C_HEADS, C_HEAD_DIM).astype(k.dtype)
    v_past = jnp.take(pool_v, page_table, axis=0).reshape(N, past, C_HEADS, C_HEAD_DIM).astype(v.dtype)
    k_all = jnp.concatenate([k_past, k], axis=1)
    v_all = jnp.concatenate([v_past, v], axis=1)
    k_pos = jnp.arange(past + L, dtype=jnp.int32)
    q_pos = past + jnp.arange(L, dtype=jnp.int32)
    o = stick_breaking_blocks(q, k_all, v_all, bias, q_pos, k_pos)
    return o.reshape(N, L, C_WIDTH) @ w_out, k, v

def setup_inputs(seed: int = 0) -> dict:
    key = jax.random.key(seed)
    ks = jax.random.split(key, 24)
    f32 = jnp.float32
    n = lambda i, shape: jax.random.normal(ks[i], shape, f32)
    n_pages = PAST_LEN // PAGE_SIZE
    n_pool = (DEC_BATCH * n_pages * 5) // 4
    page_table = jax.random.permutation(ks[5], n_pool)[:DEC_BATCH * n_pages].reshape(DEC_BATCH, n_pages).astype(jnp.int32)
    return {
        'x_prompt': n(0, (BATCH, SEQ, D_MODEL)),
        'x_sample': n(1, (DEC_BATCH, DEC_SEQ, D_MODEL)),
        'state_b': n(2, (N_EVEN, DEC_BATCH, B_HEADS, B_HEAD_DIM, B_HEAD_DIM)),
        'cache_k': n(3, (N_ODD, n_pool, PAGE_SIZE, C_HEADS, C_HEAD_DIM)),
        'cache_v': n(4, (N_ODD, n_pool, PAGE_SIZE, C_HEADS, C_HEAD_DIM)),
        'page_table': page_table,
        'ab_w_in': n(6, (N_EVEN, D_MODEL, AB_IN)) * D_MODEL ** -0.5,
        'ab_w_out': n(7, (N_EVEN, A_WIDTH + B_WIDTH, D_MODEL)) * ((A_WIDTH + B_WIDTH) ** -0.5 * DN_BETA),
        'a_w_s': n(8, (N_EVEN, A_HEADS, A_CHUNK, A_CHUNK)) * A_CHUNK ** -0.5,
        'a_b_s': 1.0 + 0.1 * n(9, (N_EVEN, A_HEADS, A_CHUNK)),
        'a_ln_g': 1.0 + 0.1 * n(10, (N_EVEN, A_WIDTH)),
        'a_ln_b': 0.1 * n(11, (N_EVEN, A_WIDTH)),
        'b_lb_logits': 0.5 * n(12, (DEPTH + 1, B_WIDTH)),
        'b_norm_g': 1.0 + 0.1 * n(13, (N_EVEN, B_HEAD_DIM)),
        'c_w_in': n(14, (N_ODD, D_MODEL, 3 * C_WIDTH)) * D_MODEL ** -0.5,
        'c_w_out': n(15, (N_ODD, C_WIDTH, D_MODEL)) * (C_WIDTH ** -0.5 * DN_BETA),
        'c_logit_bias': C_BIAS_INIT + 0.3 * n(23, (N_ODD, C_HEADS)),
        'ln1_g': 1.0 + 0.1 * n(16, (DEPTH, D_MODEL)),
        'ln1_b': 0.1 * n(17, (DEPTH, D_MODEL)),
        'ln2_g': 1.0 + 0.1 * n(18, (DEPTH, D_MODEL)),
        'ln2_b': 0.1 * n(19, (DEPTH, D_MODEL)),
        'ffn_w_gate': n(20, (DEPTH, D_MODEL, FFN_HIDDEN)) * D_MODEL ** -0.5,
        'ffn_w_up': n(21, (DEPTH, D_MODEL, FFN_HIDDEN)) * D_MODEL ** -0.5,
        'ffn_w_down': n(22, (DEPTH, FFN_HIDDEN, D_MODEL)) * (FFN_HIDDEN ** -0.5 * DN_BETA),
    }

def reference(x_prompt, x_sample, state_b, cache_k, cache_v, page_table, ab_w_in, ab_w_out, a_w_s, a_b_s, a_ln_g, a_ln_b, b_lb_logits, b_norm_g, c_w_in, c_w_out, c_logit_bias, ln1_g, ln1_b, ln2_g, ln2_b, ffn_w_gate, ffn_w_up, ffn_w_down):
    hp, hs = x_prompt, x_sample
    lower_bounds = jnp.cumsum(jax.nn.softmax(b_lb_logits.astype(jnp.float32), axis=0), axis=0)
    a_v_s, b_p, b_s, k_p, v_p, k_s, v_s = [], [], [], [], [], [], []
    for layer in range(DEPTH):
        i = layer // 2
        if layer % 2 == 0:
            ab = (ab_w_in[i], ab_w_out[i], a_w_s[i], a_b_s[i], a_ln_g[i], a_ln_b[i], lower_bounds[layer], b_norm_g[i])
            s0 = jnp.zeros((hp.shape[0], B_HEADS, B_HEAD_DIM, B_HEAD_DIM), jnp.float32)
            mp, _, sp = mixer_ab(hp, s0, *ab)
            ms, av, ss = mixer_ab(hs, state_b[i], *ab)
            a_v_s.append(av)
            b_p.append(sp)
            b_s.append(ss)
        else:
            mp, kp, vp = mixer_c_prompt(hp, c_w_in[i], c_w_out[i], c_logit_bias[i])
            ms, kn, vn = mixer_c_sample(hs, cache_k[i], cache_v[i], page_table, c_w_in[i], c_w_out[i], c_logit_bias[i])
            k_p.append(kp)
            v_p.append(vp)
            k_s.append(kn)
            v_s.append(vn)
        hp = layer_norm(DN_ALPHA * hp + mp, ln1_g[layer], ln1_b[layer])
        hs = layer_norm(DN_ALPHA * hs + ms, ln1_g[layer], ln1_b[layer])
        hp = layer_norm(DN_ALPHA * hp + swiglu(hp, ffn_w_gate[layer], ffn_w_up[layer], ffn_w_down[layer]), ln2_g[layer], ln2_b[layer])
        hs = layer_norm(DN_ALPHA * hs + swiglu(hs, ffn_w_gate[layer], ffn_w_up[layer], ffn_w_down[layer]), ln2_g[layer], ln2_b[layer])
    state_a_v_sample = jnp.stack(a_v_s)
    state_b_prompt = jnp.stack(b_p)
    state_b_sample = jnp.stack(b_s)
    cache_k_prompt = jnp.stack(k_p)
    cache_v_prompt = jnp.stack(v_p)
    cache_k_sample = jnp.stack(k_s)
    cache_v_sample = jnp.stack(v_s)
    return (hp, hs, state_a_v_sample, state_b_prompt, state_b_sample, cache_k_prompt, cache_v_prompt, cache_k_sample, cache_v_sample)


_drawn_inputs = setup_inputs


def setup_inputs(seed=0):
    import zlib

    import numpy as np

    out = dict(_drawn_inputs(seed))
    spreads = {}
    factors = {'cache_k': 4.111, 'cache_v': 3.335, 'a_b_s': 2.845, 'b_norm_g': 3.702, 'c_logit_bias': 8.0}
    for name, (base, spread) in spreads.items():
        noise = np.random.default_rng([zlib.crc32(name.encode()), seed]).standard_normal(out[name].shape)
        drawn = base * np.exp(spread * noise) if base else spread * noise
        out[name] = jnp.asarray(drawn.astype(out[name].dtype))
    for name, factor in factors.items():
        out[name] = (out[name] * factor).astype(out[name].dtype)
    return out
```

```python
from contextlib import ExitStack

import concourse.bass as bass
from concourse import mybir

F32 = mybir.dt.float32
F32R = mybir.dt.float32r
I32 = mybir.dt.int32
ALU = mybir.AluOpType
ACT = mybir.ActivationFunctionType
AX = mybir.AxisListType.X

P = 128
D = 1024
KD = D // P
SEQ = 1024
DEC = 8
DQ = 4
NS = DEC * DQ
T = SEQ + NS
NP = SEQ // P
CW = T // 3
CH = [slice(c * CW, (c + 1) * CW) for c in range(3)]
HB = 4
FFN = 2816
NF = FFN // P
GROUPS = [(0, 8), (8, 8), (16, 6)]
PAGES = 8
NPAIR = 8
LEVELS = [64, 32, 16, 8, 4, 2, 1]
LAYERS = 2
ALPHA = 4.0 ** 0.25
LN_EPS = 1e-5
RMS_EPS = 1e-6
MASKED = -30000.0
ZCAP = 40.0

AB_TILES = 6 * HB
TB = {"ab": 0, "about": AB_TILES}
_n = AB_TILES + KD
for _l in range(2):
    if _l == 1:
        TB["c"] = _n
        _n += 3 * NPAIR
        TB["cout"] = _n
        _n += KD
    for _g, (_b, _k) in enumerate(GROUPS):
        TB["up", _l, _g] = _n
        _n += 2 * _k
        TB["down", _l, _g] = _n
        _n += KD
N_TILES = _n
SLOT_LOADS = {}
for _s, _t in TB.items():
    late = _t > TB["c"]
    SLOT_LOADS[_s] = (_t // 2 + (NPAIR // 2 if late else 0), _t // 2 - (NPAIR // 2 if late else 0))


def hybrid_step(nc, x_prompt, x_sample, state_b, cache_k, cache_v, page_table, ab_w_in, ab_w_out, a_w_s, a_b_s,
                a_ln_g, a_ln_b, b_lb_logits, b_norm_g, c_w_in, c_w_out, c_logit_bias, ln1_g, ln1_b, ln2_g, ln2_b,
                ffn_w_gate, ffn_w_up, ffn_w_down, y_prompt, y_sample, a_v_sample, state_b_prompt, state_b_sample,
                ck_prompt, cv_prompt, ck_sample, cv_sample):
    ctx = ExitStack()
    with ctx:
        def sem(name):
            return ctx.enter_context(nc.semaphore(name))

        def place(stack, name, shape, dt=F32):
            return stack.enter_context(nc.sbuf_tensor(name, shape, dt))

        XH = place(ctx, "XH", [P, KD, T], F32R)
        XL = place(ctx, "XL", [P, KD, T], F32R)
        R = place(ctx, "R", [P, KD, T])
        RAW = [place(ctx, f"RAW{s}", [P, KD, P]) for s in range(2)]
        WH = [place(ctx, f"WH{s}", [P, KD, P], F32R) for s in range(2)]
        WL = [place(ctx, f"WL{s}", [P, KD, P], F32R) for s in range(2)]
        ident = place(ctx, "ident", [P, P])
        ones = place(ctx, "ones", [P, P])
        tri = place(ctx, "tri", [P, P])
        triR = place(ctx, "triR", [P, P], F32R)
        restR = place(ctx, "restR", [P, P], F32R)
        zero = place(ctx, "zero", [P, 1])
        epsln = place(ctx, "epsln", [P, 1])
        epsrms = place(ctx, "epsrms", [P, 1])
        lnp = place(ctx, "lnp", [P, 4, 2, KD])
        lbp = place(ctx, "lbp", [P, 16])
        lbw = place(ctx, "lbw", [P, 40])
        cbias = place(ctx, "cbias", [P, 16])

        with ExitStack() as s:
            levmask = place(s, "levmask", [P, 7, P])
            resets = place(s, "resets", [P, T])
            credit = place(s, "credit", [P, 24])
            pad = place(s, "pad", [P, 9])
            sel = place(s, "sel", [NS, DEC])
            WT = place(s, "WT", [P, HB, P])
            WS = place(s, "WS", [NS, HB, NS])
            bsrow = place(s, "bsrow", [1, HB, P])
            bsS = place(s, "bsS", [1, HB, DEC, DQ])
            gainA = place(s, "gainA", [P, HB, P])
            biasA = place(s, "biasA", [P, HB, P])
            U = place(s, "U", [P, T])
            V = place(s, "V", [P, T])
            VT = place(s, "VT", [P, NP + 1, P])
            Q = place(s, "Q", [P, T])
            K = place(s, "K", [P, T])
            G = place(s, "G", [P, T])
            EX = [place(s, f"EX{i}", [P, T]) for i in range(2)]
            VB = place(s, "VB", [P, NP + 1, P])
            SGG = place(s, "SGG", [P, T])
            SC = place(s, "SC", [P, NP + 1, P])
            KT = place(s, "KT", [P, NP + 1, P])
            SS = place(s, "SS", [P, NP, P])
            S0 = place(s, "S0", [P, DEC, P])
            DG = place(s, "DG", [P, 2, 8])
            bst = place(s, "bst", [P, NP + 1, 6])
            bmv = place(s, "bmv", [P, NP + 1, 2])
            brs = place(s, "brs", [P, NP + 1])
        VX = V[0:NS, 0:DEC * P].rearrange("p (n v) -> p n v", n=DEC)
        XS = U[0:NS, 0:D]
        with ExitStack() as s:
            QH, QL, KH, KL = (place(s, n, [P, T], F32R) for n in ("QH", "QL", "KH", "KL"))
            KF = place(s, "KF", [P, T])
            VI = place(s, "VI", [P, T])
            KTOK = place(s, "KTOK", [P, NP + 1, P])
            VTOK = place(s, "VTOK", [P, NP + 1, P])
            Z = [place(s, f"Z{i}", [P, 512]) for i in range(4)]
            E = [place(s, f"E{i}", [P, 512]) for i in range(2)]
            SPH = [place(s, f"SPH{i}", [P, 512], F32R) for i in range(2)]
            SPL = [place(s, f"SPL{i}", [P, 512], F32R) for i in range(2)]
            KP = [place(s, f"KP{i}", [P, PAGES, P]) for i in range(2)]
            VP = [place(s, f"VP{i}", [P, PAGES, P]) for i in range(2)]
            KTP = [place(s, f"KTP{i}", [P, 512]) for i in range(2)]
            DZ = place(s, "DZ", [P, DEC, PAGES, 2, DQ])
            DE = place(s, "DE", [P, DEC, PAGES, 2, DQ])
            DSUF = place(s, "DSUF", [P, DEC, PAGES, 2 * DQ])
            QD = place(s, "QD", [P, DEC, 2, DQ])
            NZ = place(s, "NZ", [NS, DEC, 2, DQ])
            NE = place(s, "NE", [NS, DEC, 2, DQ])
            pbias = place(s, "pbias", [P, 2])
            cap = place(s, "cap", [P, P])
            capnew = place(s, "capnew", [NS, DEC, 2, DQ])
            pt = place(s, "pt", [1, DEC * PAGES], I32)
        with ExitStack() as s:
            HH = place(s, "HH", [P, KD, T], F32R)
            HL = place(s, "HL", [P, KD, T], F32R)
            SG = [place(s, f"SG{i}", [P, CW]) for i in range(3)]
            HF = [place(s, f"HF{i}", [P, CW]) for i in range(3)]
        with ExitStack() as s:
            SQ = [place(s, f"SQ{i}", [P, KD, CW]) for i in range(2)]
            LS = place(s, "LS", [P, T])
            RS = place(s, "RS", [P, T])
            YT = [place(s, f"YT{i}", [P, D]) for i in range(2)]

        banks = [ctx.enter_context(nc.psum_tensor(f"bank{i}", [P, 512], F32)) for i in range(8)]

        w_raw = [sem(f"w_raw{s}") for s in range(2)]
        w_split = sem("w_split")
        d_mm = sem("d_mm")
        d_ev = sem("d_ev")
        par_load = sem("par_load")
        x_load = sem("x_load")
        set_pool = sem("set_pool")
        set_dve = sem("set_dve")
        xt_mm = sem("xt_mm")
        xt_hi = sem("xt_hi")
        xt_lo = sem("xt_lo")
        par_mm = sem("par_mm")
        par_ev = sem("par_ev")
        wt_done = sem("wt_done")
        ws_load = sem("ws_load")
        lb_max = sem("lb_max")
        lb_exp = sem("lb_exp")
        lb_own = sem("lb_own")
        s0_load = sem("s0_load")
        q_act = sem("q_act")
        sig_ready = sem("sig_ready")
        f_ready = sem("f_ready")
        k_ready = sem("k_ready")
        g_ready = sem("g_ready")
        diff_ready = sem("diff_ready")
        exp_ready = sem("exp_ready")
        x_ready = sem("x_ready")
        lev_mm = sem("lev_mm")
        lev_read = sem("lev_read")
        sc_zero = sem("sc_zero")
        vi_tr = sem("vi_tr")
        vb_ready = sem("vb_ready")
        vx_ready = sem("vx_ready")
        kt_tr = sem("kt_tr")
        kt_ready = sem("kt_ready")
        kv_mm = sem("kv_mm")
        st_chain = sem("st_chain")
        skv_mm = sem("skv_mm")
        sst_own = sem("sst_own")
        o_mm = sem("o_mm")
        o_ev = sem("o_ev")
        osq = sem("osq")
        ms_mm = sem("ms_mm")
        rms_std = sem("rms_std")
        o_own = sem("o_own")
        b_done = sem("b_done")
        u_act = sem("u_act")
        v_act = sem("v_act")
        sg_act = sem("sg_act")
        v_tr = sem("v_tr")
        v_stat = sem("v_stat")
        v_std = sem("v_std")
        v_own = sem("v_own")
        vt_ready = sem("vt_ready")
        sv_mm = sem("sv_mm")
        a_done = sem("a_done")
        ab_out = sem("ab_out")
        pt_load = sem("pt_load")
        at_pool = sem("at_pool")
        at_zero = sem("at_zero")
        q_hi = sem("q_hi")
        k_hi = sem("k_hi")
        qk_free = sem("qk_free")
        v_free = sem("v_free")
        kp_load = [sem(f"kp_load{i}") for i in range(2)]
        vp_load = [sem(f"vp_load{i}") for i in range(2)]
        kp_tr = sem("kp_tr")
        kp_ev = sem("kp_ev")
        kp_z = sem("kp_z")
        ktok_tr = sem("ktok_tr")
        ktok_ev = sem("ktok_ev")
        vtok_tr = sem("vtok_tr")
        vtok_ev = sem("vtok_ev")
        kv_store = sem("kv_store")
        pb_ready = sem("pb_ready")
        zn_mm = sem("zn_mm")
        nz_ready = sem("nz_ready")
        nz_own = sem("nz_own")
        ne_min = sem("ne_min")
        ne_act = sem("ne_act")
        nsp_ready = sem("nsp_ready")
        rn_mm = sem("rn_mm")
        narg = sem("narg")
        nw_ready = sem("nw_ready")
        dz_ready = sem("dz_ready")
        de_min = sem("de_min")
        de_act = sem("de_act")
        dsp_ready = sem("dsp_ready")
        dsuf = sem("dsuf")
        rd_mm = sem("rd_mm")
        darg = sem("darg")
        dw_ready = sem("dw_ready")
        dv_mm = sem("dv_mm")
        do_ev = sem("do_ev")
        z_mm = sem("z_mm")
        zc = sem("zc")
        capped = sem("capped")
        e_min = sem("e_min")
        e_exp = sem("e_exp")
        e_ln = sem("e_ln")
        sp_ready = sem("sp_ready")
        sph_ready = sem("sph_ready")
        spl_ready = sem("spl_ready")
        tri_mm = sem("tri_mm")
        arg_ready = sem("arg_ready")
        carry_mm = sem("carry_mm")
        w_ready = sem("w_ready")
        pv_mm = sem("pv_mm")
        po_ev = sem("po_ev")

        m_hi = sem("m_hi")
        m_lo = sem("m_lo")
        res1 = sem("res1")
        res = sem("res")
        gate_read = sem("gate_read")
        up_read = sem("up_read")
        h_hi = sem("h_hi")
        h_lo = sem("h_lo")
        ln_sum = sem("ln_sum")
        ln_mean = sem("ln_mean")
        ln_cent = sem("ln_cent")
        ln_sq = sem("ln_sq")
        ln_sum2 = sem("ln_sum2")
        ln_var = sem("ln_var")
        ln_std = sem("ln_std")
        ln_rstd = sem("ln_rstd")
        ln_norm = sem("ln_norm")
        ln_aff = sem("ln_aff")
        x_hi = sem("x_hi")
        x_lo = sem("x_lo")
        y_tr = sem("y_tr")
        y_ev = sem("y_ev")
        y_out = [sem(f"y_out{i}") for i in range(2)]

        out_stages = []
        for l in range(2):
            out_stages.append((("about", "cout")[l], KD, HH, None, l))
            out_stages += [(("down", l, g), k, HH, g, l) for g, (_, k) in enumerate(GROUPS)]
        units, scaled, n1, n2 = {}, {}, 0, 0
        for name, _, _, g, _ in out_stages:
            units[name], scaled[name] = n1, n2
            n1 += 3 * KD
            n2 += 3 * KD if not g else 0
        ln_units = {}
        for n, name in enumerate(["about", ("down", 0, 2), "cout", ("down", 1, 2)]):
            ln_units[n] = (units[name] + 3 * KD, scaled[name] + (3 * KD if n % 2 == 0 else 0))
        ffn_pairs = {}
        n1 = 0
        for l in range(2):
            for g, (_, k) in enumerate(GROUPS):
                ffn_pairs[l, g] = n1
                n1 += k

        STEPS = [(h, c, b) for h in range(2) for c in (1, 0) for b in range(4 * c + 3, -1, -1)]
        NST = len(STEPS)
        LOW = [max(b * P - 512 * c, 0) for _, c, b in STEPS]
        DIAG = [b >= 4 * c for _, c, b in STEPS]
        FIRST = [b == 4 * c + 3 for _, c, b in STEPS]
        FINAL = [b == 0 for _, c, b in STEPS]
        carries = lambda s: sum(not f for f in FINAL[:s + 1])
        NCARRY = carries(NST - 1)
        chunks_done = lambda s: sum(FINAL[:s + 1])
        ck_v = cache_k[0].rearrange("g p h d -> g p (h d)")
        cv_v = cache_v[0].rearrange("g p h d -> g p (h d)")
        N_POOL = cache_k.shape[1]
        ckp_v, cvp_v = (a[0, 0].rearrange("(n p) h d -> p n (h d)", p=P) for a in (ck_prompt, cv_prompt))
        cks_v, cvs_v = (a[0].rearrange("n t h d -> (n t) (h d)") for a in (ck_sample, cv_sample))

        GROUPS_AT = ((0, 1, 2), (3, 4, 5), (6, 7, 8), (9, 10, 11), (12, 13), (14, 15))
        LAST_LN = 2 * LAYERS - 1
        VBANK = (6, 7)
        VARB = (6, 7, 3)
        AB_COLS = (8, 12, 16, 20, 0, 4)
        PROWS, LROWS, BROW = EX[0][0:64, 0:P], EX[1][0:13, 0:P], Q[0:1, 0:1040]
        s0_v = state_b[0].rearrange("n h k v -> k h n v")
        s0o_v = state_b_sample[0].rearrange("n h k v -> k h n v")
        av_v = a_v_sample[0].rearrange("n t (h d) -> (n t) h d", h=HB)
        sbp_v = state_b_prompt[0, 0].rearrange("h k v -> k h v")

        block = ctx.enter_context(nc.Block())
        flat = lambda a: a.rearrange("p k t -> p (k t)")
        wv = lambda w, l: w[l].rearrange("(k p) (n c) -> p n k c", p=P, c=P)
        w_ab, w_abo = wv(ab_w_in, 0), wv(ab_w_out, 0)
        w_c, w_co = wv(c_w_in, 0), wv(c_w_out, 0)
        w_gate, w_up, w_down = ([wv(w, l) for l in range(2)] for w in (ffn_w_gate, ffn_w_up, ffn_w_down))
        XP = flat(R)[:, 0:NP * D].rearrange("p (n d) -> p n d", n=NP)

        @block.sync
        def _(sp):
            for k in range(NP):
                sp.dma_start(XP[:, k, :], x_prompt[0, k * P:(k + 1) * P, :]).then_inc(x_load, 16)
            sp.dma_start(XS, x_sample.rearrange("n t d -> (n t) d")).then_inc(x_load, 16)
            for i, w in enumerate((ln1_g, ln1_b, ln2_g, ln2_b)):
                sp.dma_start(PROWS[16 * i:16 * i + 16, :], w.rearrange("l (k p) -> (l k) p", p=P)).then_inc(par_load, 16)
            sp.dma_start(LROWS[0:12, :], b_lb_logits.rearrange("r (h p) -> (r h) p", p=P)).then_inc(par_load, 16)
            sp.dma_start(LROWS[12:13, :], b_norm_g).then_inc(par_load, 16)
            sp.dma_start(BROW[:, 0:512], a_ln_g).then_inc(par_load, 16)
            sp.dma_start(BROW[:, 512:1024], a_ln_b).then_inc(par_load, 16)
            sp.dma_start(BROW[:, 1024:1040], c_logit_bias).then_inc(par_load, 16)
            sp.dma_start(KT[:, 0:HB, :], a_w_s[0].rearrange("h t s -> t h s")).then_inc(par_load, 16)
            sp.dma_start(bsrow[:], a_b_s).then_inc(par_load, 16)
            sp.wait_ge(wt_done, 1)
            for n in range(DEC):
                sp.dma_start(WS[DQ * n:DQ * n + DQ, :, DQ * n:DQ * n + DQ], WT[0:DQ, :, 0:DQ]).then_inc(ws_load, 16)

            def stream(stage, pairs, kb, k0, cols, first=0):
                with sp.Fori(first, pairs) as j:
                    for s in range(2):
                        w, col = cols(j, s)
                        col = sp.snap(col)
                        sp.wait_ge(w_split, 2 * TB[stage] + 4 * j + 2 * s + 1)
                        sp.dma_start(RAW[s][:, 0:kb, :], w[:, bass.ds(col, 1), k0:k0 + kb]
                                     .rearrange("p n k c -> p (n k) c")).then_inc(w_raw[s], 16)

            def attention_loads():
                base = TB["c"]

                def tile(hp, j, nxt):
                    col = sp.snap(hp + nxt + NPAIR * j)
                    sp.wait_ge(w_split, 2 * base + 6 * (hp + nxt) + 2 * j + (2 if j == 0 else 0) + 1)
                    sp.dma_start(RAW[j % 2][:], w_c[:, bass.ds(col, 1)].rearrange("p n k c -> p (n k) c"))\
                      .then_inc(w_raw[j % 2], 16)

                def pages(hp, m, s, view, to, loaded, used, per):
                    _, ids = nc.values_load_multi_w_load_instructions(
                        pt[0:1, bass.ds(2 * PAGES * m + PAGES * s, PAGES)], engines=[mybir.EngineType.SP], min_val=0, max_val=N_POOL - 1)
                    first = sp.snap(hp * P)
                    sp.wait_ge(used, per * (DEC * hp + 2 * m + s) + 1)
                    for g in range(PAGES):
                        sp.dma_start(to[s][:, g, :], view[bass.ds(ids[g], 1), :, bass.ds(first, P)]
                                     .rearrange("o p c -> (o p) c")).then_inc(loaded[s], 16)

                def k_pages(hp, m, s):
                    pages(hp, m, s, ck_v, KP, kp_load, kp_tr, 2)

                def v_pages(hp, m, s):
                    pages(hp, m, s, cv_v, VP, vp_load, dv_mm, 1)

                def pair(hp, last):
                    tile(hp, 2, 0)
                    with sp.Fori(1, DEC // 2) as m:
                        for s in range(2):
                            k_pages(hp, m, s)
                    for s in range(2):
                        v_pages(hp, 0, s)
                    if last:
                        for j in range(2):
                            sp.wait_ge(w_split, 2 * TB["cout"] + 2 * j + (2 if j == 0 else 0) + 1)
                            sp.dma_start(RAW[j][:], w_co[:, j]).then_inc(w_raw[j], 16)
                    else:
                        for j in range(2):
                            tile(hp, j, 1)
                    for a, b, tok, ev in ((ckp_v, cks_v, KTOK, ktok_ev), (cvp_v, cvs_v, VTOK, vtok_ev)):
                        sp.wait_ge(pt_load, 16)
                        sp.wait_ge(ev, 3 * hp + 3)
                        sp.dma_start(a[:, :, bass.ds(2 * hp * (P // 2), P)], tok[:, 0:NP, :]).then_inc(kv_store, 16)
                        sp.dma_start(b[:, bass.ds(2 * hp * (P // 2), P)], tok[0:NS, NP, :]).then_inc(kv_store, 16)
                    with sp.Fori(1, DEC // 2) as m:
                        for s in range(2):
                            v_pages(hp, m, s)
                    if not last:
                        for s in range(2):
                            k_pages(hp + 1, 0, s)

                for j in range(2):
                    tile(0, j, 0)
                sp.wait_ge(at_pool, 3)
                sp.dma_start(pt[:], page_table.rearrange("(o n) g -> o (n g)", o=1)).then_inc(pt_load, 16)
                sp.wait_ge(pt_load, 16)
                for s in range(2):
                    k_pages(0, 0, s)
                with sp.Fori(0, NPAIR - 1) as hp:
                    pair(hp, False)
                pair(NPAIR - 1, True)

            with sp.Fori(0, HB) as h:
                for j, first in enumerate(AB_COLS):
                    col = sp.snap(h + first)
                    sp.wait_ge(w_split, 12 * h + 2 * j + 1)
                    sp.dma_start(RAW[j % 2][:], w_ab[:, bass.ds(col, 1)].rearrange("p n k c -> p (n k) c"))\
                      .then_inc(w_raw[j % 2], 16)
            for l in range(LAYERS):
                if l == 0:
                    stream("about", KD // 2, KD, 0, lambda j, s: (w_abo, 2 * j + s))
                else:
                    attention_loads()
                    stream("cout", KD // 2, KD, 0, lambda j, s: (w_co, 2 * j + s), 1)
                for g, (b0, k) in enumerate(GROUPS):
                    stream(("up", l, g), k, KD, 0, lambda j, s: ((w_gate[l], w_up[l])[s], j + b0))
                    stream(("down", l, g), KD // 2, k, b0, lambda j, s: (w_down[l], 2 * j + s))

            for n in range(NP + 1):
                sp.wait_ge(y_ev, 2 * n + 2)
                rows = P if n < NP else NS
                to = y_prompt[0, n * P:(n + 1) * P, :] if n < NP else y_sample.rearrange("n t d -> (n t) d")
                sp.dma_start(to, YT[n % 2][0:rows, :]).then_inc(y_out[n % 2], 16)
            sp.wait_ge(y_out[0], 16 * (NP // 2 + 1))
            sp.wait_ge(y_out[1], 16 * (NP // 2))
            sp.wait_ge(ab_out, 48 * HB + 16)

        @block.gpsimd
        def _(pool):
            nc.gpsimd.memset(zero[:], 0.0).then_inc(set_pool, 1)
            nc.gpsimd.memset(ident[:], 0.0).then_inc(set_pool, 1)
            nc.gpsimd.memset(tri[:], 1.0).then_inc(set_pool, 1)
            nc.gpsimd.memset(levmask[:], 0.0).then_inc(set_pool, 1)
            nc.gpsimd.memset(sel[:], 1.0).then_inc(set_pool, 1)
            nc.gpsimd.memset(WS[:], 0.0).then_inc(set_pool, 1)
            pool.wait_ge(set_pool, 6)
            nc.gpsimd.affine_select(out=ident[:], in_=ident[:], compare_op=ALU.not_equal, fill=1.0, base=0,
                                    pattern=[[-1, P]], channel_multiplier=1).then_inc(set_pool, 1)
            nc.gpsimd.affine_select(out=tri[:], in_=tri[:], compare_op=ALU.is_ge, fill=0.0, base=0,
                                    pattern=[[-1, P]], channel_multiplier=1).then_inc(set_pool, 1)
            nc.gpsimd.affine_select(out=sel[:], in_=sel[:], compare_op=ALU.is_ge, fill=0.0, base=0,
                                    pattern=[[-DQ, DEC]], channel_multiplier=1).then_inc(set_pool, 1)
            pool.wait_ge(set_pool, 9)
            nc.gpsimd.affine_select(out=sel[:], in_=sel[:], compare_op=ALU.is_ge, fill=0.0, base=DQ - 1,
                                    pattern=[[DQ, DEC]], channel_multiplier=-1).then_inc(set_pool, 1)
            for i, w in enumerate(LEVELS):
                late = levmask[:, i, :].rearrange("p (n a r) -> p n a r", a=2, r=w)[:, :, 1, :]
                nc.gpsimd.memset(late, 1.0).then_inc(set_pool, 1)
            pool.wait_ge(set_pool, 17)
            for i, w in enumerate(LEVELS):
                late = levmask[:, i, :].rearrange("p (n a r) -> p n a r", a=2, r=w)[:, :, 1, :]
                nb = P // (2 * w)
                nc.gpsimd.affine_select(out=late, in_=late, compare_op=ALU.is_ge, fill=0.0, base=0,
                                        pattern=[[-2 * w, nb], [0, w]], channel_multiplier=1).then_inc(set_pool, 1)
                pool.wait_ge(set_pool, 18 + 2 * i)
                nc.gpsimd.affine_select(out=late, in_=late, compare_op=ALU.is_ge, fill=0.0, base=w - 1,
                                        pattern=[[2 * w, nb], [0, w]], channel_multiplier=-1).then_inc(set_pool, 1)
            pool.wait_ge(par_ev, 5)
            nc.gpsimd.affine_select(out=WT[:], in_=WT[:], compare_op=ALU.is_ge, fill=0.0, base=0,
                                    pattern=[[0, HB], [1, P]], channel_multiplier=-1).then_inc(wt_done, 1)

            def split(slot, kb, loads, before, used):
                pool.wait_ge(w_raw[slot], 16 * loads)
                pool.wait_ge(d_mm, 3 * used + 1)
                nc.gpsimd.tensor_tensor(WH[slot][:, 0:kb, :], RAW[slot][:, 0:kb, :],
                                        zero[:].to_broadcast([P, kb, P]), ALU.add).then_inc(w_split, 1)
                pool.wait_ge(w_split, before + 3 + 1)
                nc.gpsimd.tensor_tensor(WL[slot][:, 0:kb, :], RAW[slot][:, 0:kb, :],
                                        WH[slot][:, 0:kb, :].bitcast(F32), ALU.subtract).then_inc(w_split, 1)

            def splits(stage, pairs, kb, first=0):
                n = TB[stage]
                l0, l1 = SLOT_LOADS[stage]
                with pool.Fori(first, pairs) as j:
                    split(0, kb, l0 + j + 1, 2 * n + 4 * j, n + 2 * j)
                    split(1, kb, l1 + j + 1, 2 * n + 4 * j + 2, n + 2 * j + 1)

            with pool.Fori(0, HB) as h:
                for j in range(6):
                    split(j % 2, KD, 3 * h + j // 2 + 1, 12 * h + 2 * j, 6 * h + j)

            def attention_pool():
                pool.wait_ge(ln_norm, 6)
                nc.gpsimd.memset(cap[:], 1e30).then_inc(at_pool, 1)
                nc.gpsimd.memset(capnew[:], 1e30).then_inc(at_pool, 1)
                nc.gpsimd.memset(QD[:], 0.0).then_inc(at_pool, 1)
                pool.wait_ge(at_pool, 3)
                nc.gpsimd.affine_select(out=cap[:], in_=cap[:], compare_op=ALU.is_ge, fill=MASKED, base=-1,
                                        pattern=[[1, P]], channel_multiplier=-1).then_inc(at_pool, 1)
                for h in range(2):
                    nc.gpsimd.affine_select(out=capnew[:, :, h, :], in_=capnew[:, :, h, :], compare_op=ALU.is_ge, fill=MASKED,
                                            base=0, pattern=[[-DQ, DEC], [0, DQ]], channel_multiplier=1).then_inc(at_pool, 1)
                pool.wait_ge(at_pool, 6)
                for h in range(2):
                    nc.gpsimd.affine_select(out=capnew[:, :, h, :], in_=capnew[:, :, h, :], compare_op=ALU.is_ge, fill=MASKED,
                                            base=-1, pattern=[[DQ, DEC], [1, DQ]], channel_multiplier=-1).then_inc(at_pool, 1)
                n0 = TB["c"]
                l0, l1 = SLOT_LOADS["c"]
                split(0, KD, l0 + 1, 2 * n0, n0 + 1)
                split(1, KD, l1 + 1, 2 * n0 + 2, n0 + 1)
                with pool.Fori(0, NPAIR) as hp:
                    n = n0 + 3 * hp
                    split(0, KD, l0 + 2 * hp + 2, 2 * n + 4, n + 2)
                    for s in range(NST):
                        c = slice(LOW[s], 512)
                        pool.wait_ge(sph_ready, NST * hp + s + 1)
                        if s >= 2:
                            if FINAL[s - 2]:
                                pool.wait_ge(tri_mm, NST * hp + s - 1)
                            else:
                                pool.wait_ge(carry_mm, NCARRY * hp + carries(s - 2))
                        nc.gpsimd.tensor_tensor(SPL[s % 2][:, c], E[s % 2][:, c], SPH[s % 2][:, c].bitcast(F32),
                                                ALU.subtract).then_inc(spl_ready, 1)
                    split(0, KD, l0 + 2 * hp + 3, 2 * n + 6, n + 4)
                    split(1, KD, l1 + hp + 2, 2 * n + 8, n + 4)

            def norm_rest(n):
                for c in range(3):
                    pool.wait_ge(x_hi, 3 * n + c + 1)
                    nc.gpsimd.tensor_tensor(XL[:, :, CH[c]], R[:, :, CH[c]], XH[:, :, CH[c]].bitcast(F32),
                                            ALU.subtract).then_inc(x_lo, 1)

            for l in range(LAYERS):
                if l == 0:
                    splits("about", KD // 2, KD)
                else:
                    attention_pool()
                    splits("cout", KD // 2, KD, 1)
                norm_rest(2 * l)
                for g, (_, k) in enumerate(GROUPS):
                    splits(("up", l, g), k, KD)
                    splits(("down", l, g), KD // 2, k)
                if 2 * l + 1 < LAST_LN:
                    norm_rest(2 * l + 1)

        @block.scalar
        def _(act):
            for k in range(KD):
                act.wait_ge(xt_mm, k + 1)
                for i, c in enumerate((slice(0, 512), slice(512, SEQ), slice(SEQ, T))):
                    n = c.stop - c.start
                    last = nc.scalar.activation(XH[:, k, c], banks[3 * (k % 2) + i][:, 0:n], ACT.Copy)
                last.then_inc(xt_hi, 1)
            act.wait_ge(lb_max, 4)
            nc.scalar.activation(lbw[:, 4:16], lbw[:, 4:16], ACT.Exp).then_inc(lb_exp, 1)

            def copy_out(c, n, to):
                act.wait_ge(d_mm, n + c + 4 + 1)
                nc.scalar.activation(to[:, CH[c]], banks[c][:, 0:CW], ACT.Copy).then_inc(d_ev, 1)

            def level_exp(h, i):
                w = LEVELS[i] if i < 7 else P
                act.wait_ge(diff_ready, 8 * h + i + 1)
                e = EX[i % 2][:, 0:SEQ if 2 < w < P else T]
                nc.scalar.activation(e, e, ACT.Exp).then_inc(exp_ready, 1)

            with act.Fori(0, HB) as h:
                n = 18 * h
                act.wait_ge(b_done, h + 1)
                act.wait_ge(ab_out, 48 * h + 16)
                act.dma_start(S0[:], s0_v[:, bass.ds(h, 1)].rearrange("k h n v -> k (h n) v")).then_inc(s0_load, 16)
                for c in range(3):
                    copy_out(c, n, Q)
                act.wait_ge(d_ev, n + 6)
                nc.scalar.activation(Q[:], Q[:], ACT.Silu).then_inc(q_act, 1)
                for c in range(3):
                    copy_out(c, n + 3, EX[1])
                act.wait_ge(d_ev, n + 9)
                nc.scalar.activation(K[:], EX[1][:], ACT.Sigmoid, scale=-1.0).then_inc(sig_ready, 1)
                nc.scalar.activation(G[:], EX[1][:], ACT.Sigmoid).then_inc(sig_ready, 1)
                act.wait_ge(sig_ready, 2 * h + 2)
                nc.scalar.activation(EX[1][:], G[:], ACT.Ln, scale=lbw[:, bass.ds(h + 28, 1)],
                                     bias=lbw[:, bass.ds(h + 24, 1)]).then_inc(f_ready, 1)
                for c in range(3):
                    copy_out(c, n + 6, U)
                act.wait_ge(vi_tr, 3 * h + 3 + 1)
                level_exp(h, 0)
                for i in range(9):
                    if i < 6:
                        level_exp(h, i + 1)
                    copy_out(i % 3, n + 9 + i - i % 3, (SGG, U, V)[i // 3])
                act.wait_ge(lev_mm, 8 * h + 6)
                nc.scalar.activation(EX[1][:], G[:], ACT.Exp).then_inc(exp_ready, 1)
                act.wait_ge(diff_ready, 8 * h + 8)
                nc.scalar.activation(EX[0][:], EX[0][:], ACT.Exp).then_inc(exp_ready, 1)
                nc.scalar.activation(DG[:, 0, :], G[:, P - 1:SEQ:P], ACT.Exp).then_inc(exp_ready, 1)
                nc.scalar.activation(DG[:, 1, :], G[:, SEQ + DQ - 1:T:DQ], ACT.Exp).then_inc(exp_ready, 1)
                act.wait_ge(d_ev, n + 21)
                nc.scalar.activation(V[:], V[:], ACT.Gelu_apprx_tanh).then_inc(v_act, 1)
                nc.scalar.activation(U[:], U[:], ACT.Gelu_apprx_tanh).then_inc(u_act, 1)
                nc.scalar.activation(SGG[:], SGG[:], ACT.Silu).then_inc(sg_act, 1)
                act.wait_ge(v_stat, h + 1)
                nc.scalar.activation(brs[:], bmv[:, :, 1], ACT.Sqrt, bias=epsln[:]).then_inc(v_std, 1)
                act.wait_ge(vt_ready, 2 * h + 2)
                act.dma_start(av_v[:, bass.ds(h, 1)].rearrange("t h d -> t (h d)"), VT[0:NS, NP, :]).then_inc(ab_out, 16)
                act.wait_ge(st_chain, 8 * h + 8)
                act.dma_start(sbp_v[:, bass.ds(h, 1)].rearrange("k h v -> k (h v)"), SS[:, NP - 1, :]).then_inc(ab_out, 16)
                act.wait_ge(o_mm, h + 1 + 1)
                for i, (b, c) in enumerate(((6, slice(0, 512)), (7, slice(512, SEQ)), (5, slice(SEQ, T)))):
                    nc.scalar.activation(K[:, c], banks[b][:, 0:c.stop - c.start], ACT.Copy).then_inc(o_ev, 1)
                act.wait_ge(o_ev, 3 * h + 3)
                nc.scalar.activation(G[:], K[:], ACT.Square).then_inc(osq, 1)
                act.wait_ge(ms_mm, h + 1)
                for c in range(3):
                    nc.scalar.activation(Q[:, CH[c]], banks[3 + c][:, 0:CW], ACT.Sqrt, bias=epsrms[:],
                                         scale=1.0 / P).then_inc(rms_std, 1)
                act.wait_ge(sst_own, 3 * h + 3)
                act.dma_start(s0o_v[:, bass.ds(h, 1)].rearrange("k h n v -> k (h n) v"), S0[:]).then_inc(ab_out, 16)

            act.wait_ge(b_done, HB + 1)
            act.wait_ge(a_done, HB)
            act.wait_ge(ab_out, 48 * HB + 16)
            for k in range(KD):
                nc.scalar.activation(HH[:, k, :], R[:, k, :], ACT.Copy).then_inc(m_hi, 1)

            def attention_act():
                act.wait_ge(at_pool, 8)
                nc.scalar.preload_act_table_set("natural_log_exp_and_others")
                with act.Fori(0, NPAIR) as hp:
                    n = 3 * (TB["c"] + 3 * hp)
                    nc.scalar.activation(pbias[:], cbias[:, bass.ds(2 * hp, 2)], ACT.Copy).then_inc(pb_ready, 1)
                    for c in range(3):
                        act.wait_ge(d_mm, n + c + 4 + 1)
                        if c == 2:
                            for h in range(2):
                                r = slice(64 * h, 64 * h + 64)
                                nc.scalar.activation(QD[r, :, h, :], banks[2][r, CW - NS:CW].rearrange("p (n i) -> p n i", i=DQ),
                                                     ACT.Copy, scale=0.125)
                        nc.scalar.activation(QH[:, CH[c]], banks[c][:, 0:CW], ACT.Copy, scale=0.125).then_inc(q_hi, 1)
                    for c in range(3):
                        act.wait_ge(d_mm, n + 3 + c + 4 + 1)
                        nc.scalar.activation(KF[:, CH[c]], banks[c][:, 0:CW], ACT.Copy)
                        nc.scalar.activation(KH[:, CH[c]], banks[c][:, 0:CW], ACT.Copy).then_inc(k_hi, 1)
                    for c in range(3):
                        act.wait_ge(d_mm, n + 6 + c + 4 + 1)
                        nc.scalar.activation(VI[:, CH[c]], banks[c][:, 0:CW], ACT.Copy).then_inc(v_free, 1)
                    act.wait_ge(kv_store, 64 * hp + 16)
                    for b in range(2):
                        act.wait_ge(vtok_tr, 3 * hp + b + 1)
                        nc.scalar.activation(VTOK[:, 4 * b:4 * b + 4, :].rearrange("p n c -> p (n c)"), banks[6 + b][:],
                                             ACT.Copy).then_inc(vtok_ev, 1)
                    act.wait_ge(vtok_tr, 3 * hp + 3)
                    nc.scalar.activation(VTOK[0:NS, NP, :], banks[3][0:NS, 0:P], ACT.Copy).then_inc(vtok_ev, 1)
                    act.wait_ge(pb_ready, hp + 1)
                    act.wait_ge(zn_mm, hp + 1)
                    for h in range(2):
                        nc.scalar.activation(NZ[:, :, h, :], banks[4][0:NS, 0:64].rearrange("p (n h i) -> p n h i", h=2, i=DQ)[:, :, h, :],
                                             ACT.Identity, bias=pbias[0:NS, h:h + 1]).then_inc(nz_ready, 1)
                    act.wait_ge(kp_z, 16 * hp + 16)
                    for h in range(2):
                        nc.scalar.activation(DZ[:, :, :, h, :].rearrange("p n g i -> p (n g) i"),
                                             banks[5][:].rearrange("p (m h i) -> p m h i", h=2, i=DQ)[:, :, h, :],
                                             ACT.Identity, bias=pbias[:, h:h + 1]).then_inc(dz_ready, 1)
                    def logits(s):
                        if s >= 4:
                            act.wait_ge(pv_mm, NST * hp + s - 3)
                        act.wait_ge(z_mm, NST * hp + s + 1)
                        c, h = slice(LOW[s], 512), STEPS[s][0]
                        nc.scalar.activation(Z[s % 4][:, c], banks[6 + s % 2][:, c], ACT.Identity,
                                             bias=pbias[:, h:h + 1]).then_inc(zc, 1)

                    def log1p_exp(s):
                        e = E[s % 2][:, LOW[s]:512]
                        act.wait_ge(e_min, NST * hp + s + 1)
                        nc.scalar.activation(e, e, ACT.Exp).then_inc(e_exp, 1)
                        act.wait_ge(e_exp, NST * hp + s + 1)
                        nc.scalar.activation(e, e, ACT.Ln, bias=1.0).then_inc(e_ln, 1)

                    def weights(s):
                        z = Z[s % 4][:, LOW[s]:512]
                        act.wait_ge(arg_ready, NST * hp + s + 1)
                        nc.scalar.activation(z, z, ACT.Exp).then_inc(w_ready, 1)

                    def output(s):
                        h, c, _ = STEPS[s]
                        r = slice(64 * h, 64 * h + 64)
                        act.wait_ge(pv_mm, NST * hp + s + 1)
                        nc.scalar.activation(R[r, bass.ds(hp, 1), 512 * c:512 * c + 512].rearrange("p k t -> p (k t)"),
                                             banks[4][r, :], ACT.Copy).then_inc(po_ev, 1)

                    for s in range(-3, NST + 1):
                        if 0 <= s + 2 < NST:
                            log1p_exp(s + 2)
                        if 0 <= s < NST:
                            weights(s)
                        if s >= 1 and FINAL[s - 1]:
                            output(s - 1)
                        if s + 3 < NST:
                            logits(s + 3)
                        if s == -1:
                            for e, m, a in ((NE, ne_min, ne_act), (DE, de_min, de_act)):
                                act.wait_ge(m, hp + 1)
                                nc.scalar.activation(e[:], e[:], ACT.Exp).then_inc(a, 1)
                                act.wait_ge(a, 2 * hp + 1)
                                nc.scalar.activation(e[:], e[:], ACT.Ln, bias=1.0).then_inc(a, 1)
                        if s == 8:
                            act.wait_ge(narg, hp + 1 + 1)
                            nc.scalar.activation(NE[:], NZ[:], ACT.Exp).then_inc(nw_ready, 1)
                            act.wait_ge(darg, hp + 1)
                            nc.scalar.activation(DE[:], DZ[:], ACT.Exp).then_inc(dw_ready, 1)
                    act.wait_ge(dv_mm, DEC * hp + DEC + 2)
                    for h in range(2):
                        r = slice(64 * h, 64 * h + 64)
                        nc.scalar.activation(R[r, bass.ds(hp, 1), SEQ:T].rearrange("p k (n i) -> p (k n) i", i=DQ),
                                             banks[5][r, 0:64].rearrange("p (n h i) -> p n h i", h=2, i=DQ)[:, :, h, :],
                                             ACT.Copy).then_inc(do_ev, 1)
                act.wait_ge(kv_store, 64 * NPAIR + 16)
                act.wait_ge(po_ev, 4 * NPAIR + 1)
                act.wait_ge(do_ev, 2 * NPAIR + 1)
                for k in range(KD):
                    nc.scalar.activation(HH[:, k, :], R[:, k, :], ACT.Copy).then_inc(m_hi, 1)

            def norm_act(n):
                l, o = n // 2, 2 * (n % 2)
                for c in range(3):
                    act.wait_ge(ln_cent, 3 * n + c + 1)
                    if c == 2:
                        act.wait_ge(ln_sum2, 3 * n + 1)
                    nc.scalar.activation(SQ[c % 2][:], R[:, :, CH[c]], ACT.Square).then_inc(ln_sq, 1)
                for c in range(3):
                    act.wait_ge(ln_var, 3 * n + c + 1)
                    nc.scalar.activation(RS[:, CH[c]], banks[VARB[c]][:, 0:CW], ACT.Sqrt, bias=epsln[:], scale=1.0 / D).then_inc(ln_std, 1)
                for c in range(3):
                    act.wait_ge(ln_norm, 3 * n + c + 1)
                    for k in range(KD):
                        nc.scalar.activation(R[:, k, CH[c]], R[:, k, CH[c]], ACT.Identity,
                                             scale=lnp[:, o, l, k:k + 1], bias=lnp[:, o + 1, l, k:k + 1])\
                          .then_inc(ln_aff, 1)
                    if n < LAST_LN:
                        act.wait_ge(ln_aff, 24 * n + 8 * c + 8)
                        nc.scalar.activation(XH[:, :, CH[c]], R[:, :, CH[c]], ACT.Copy).then_inc(x_hi, 1)

            for l in range(LAYERS):
                if l == 1:
                    attention_act()
                norm_act(2 * l)
                for g, (_, kg) in enumerate(GROUPS):
                    done = ffn_pairs[l, g]
                    if g:
                        act.wait_ge(d_mm, 3 * (TB["down", l, g - 1] + KD) + 3 + 1)
                    with act.Fori(0, kg) as j:
                        for c in range(3):
                            act.wait_ge(d_mm, 3 * TB["up", l, g] + 6 * j + c + 4 + 1)
                            act.wait_ge(up_read, 3 * done + 3 * j + c + 1)
                            nc.scalar.activation(SG[c][:], banks[c][:, 0:CW], ACT.Silu).then_inc(gate_read, 1)
                        for c in range(3):
                            act.wait_ge(up_read, 3 * done + 3 * j + c + 4)
                            nc.scalar.activation(HH[:, bass.ds(j, 1), CH[c]].rearrange("p k t -> p (k t)"),
                                                 HF[c][:], ACT.Copy).then_inc(h_hi, 1)
                norm_act(2 * l + 1)

        @block.vector
        def _(dve):
            v = nc.vector
            v.memset(ones[:], 1.0).then_inc(set_dve, 1)
            v.memset(epsln[:], LN_EPS).then_inc(set_dve, 1)
            v.memset(epsrms[:], RMS_EPS).then_inc(set_dve, 1)
            v.memset(bmv[:], 1.0).then_inc(set_dve, 1)
            v.memset(resets[:], 1.0).then_inc(set_dve, 1)
            dve.wait_ge(set_dve, 5)
            v.memset(resets[:, 0:SEQ:P], 0.0).then_inc(set_dve, 1)
            v.memset(resets[:, SEQ:T:DQ], 0.0).then_inc(set_dve, 1)
            for i, (s, n) in enumerate(((w_split, 3), (d_mm, 4), (d_ev, 3), (res1, 3), (up_read, 3), (h_lo, 3), (lev_read, 1), (kp_tr, 3), (dv_mm, 2), (b_done, 1), (kt_tr, 1), (vi_tr, 1), (o_mm, 1), (rms_std, 1), (narg, 1), (po_ev, 1), (do_ev, 1), (ab_out, 16), (kv_store, 16), (v_free, 3))):
                v.memset(credit[:, i:i + 1], 0.0).then_inc(s, n)
            dve.wait_ge(set_pool, 31)
            v.tensor_copy(triR[:], tri[:]).then_inc(set_dve, 1)
            v.tensor_scalar(restR[:], tri[:], -1.0, 1.0, ALU.mult, ALU.add).then_inc(set_dve, 1)
            dve.wait_ge(par_mm, 5)
            v.tensor_copy(lnp[:].rearrange("p a l k -> p (a l k)"), banks[6][:, 0:64]).then_inc(par_ev, 1)
            v.tensor_copy(lbp[:, 0:13], banks[6][:, 64:77]).then_inc(par_ev, 1)
            v.tensor_copy(cbias[:], banks[6][:, 128:144]).then_inc(par_ev, 1)
            v.tensor_copy(WT[:].rearrange("p h s -> p (h s)"), banks[7][:]).then_inc(par_ev, 2)
            for k in range(KD):
                dve.wait_ge(xt_hi, k + 1)
                for i, c in enumerate((slice(0, 512), slice(512, SEQ), slice(SEQ, T))):
                    n = c.stop - c.start
                    last = v.tensor_tensor(XL[:, k, c], banks[3 * (k % 2) + i][:, 0:n], XH[:, k, c].bitcast(F32),
                                           ALU.subtract)
                last.then_inc(xt_lo, 1)
            dve.wait_ge(par_mm, 7)
            v.tensor_copy(gainA[:].rearrange("p h d -> p (h d)"), banks[6][:]).then_inc(par_ev, 1)
            v.tensor_copy(biasA[:].rearrange("p h d -> p (h d)"), banks[7][:]).then_inc(par_ev, 1)
            dve.wait_ge(par_load, 16 * 11)
            v.tensor_copy(bsS[:], bsrow[:, :, None, 0:DQ].to_broadcast([1, HB, DEC, DQ])).then_inc(par_ev, 1)
            dve.wait_ge(par_ev, 5)
            v.tensor_tensor(lbw[:, 0:4], lbp[:, 0:4], lbp[:, 4:8], ALU.max).then_inc(lb_max, 1)
            dve.wait_ge(lb_max, 1)
            v.tensor_tensor(lbw[:, 0:4], lbw[:, 0:4], lbp[:, 8:12], ALU.max).then_inc(lb_max, 1)
            dve.wait_ge(lb_max, 2)
            v.tensor_tensor(lbw[:, 4:16].rearrange("p (r h) -> p r h", r=3), lbp[:, 0:12].rearrange("p (r h) -> p r h", r=3),
                            lbw[:, None, 0:4].to_broadcast([P, 3, 4]), ALU.subtract).then_inc(lb_max, 2)
            dve.wait_ge(lb_exp, 1)
            v.tensor_tensor(lbw[:, 16:20], lbw[:, 4:8], lbw[:, 8:12], ALU.add).then_inc(lb_own, 1)
            dve.wait_ge(lb_own, 1)
            v.tensor_tensor(lbw[:, 16:20], lbw[:, 16:20], lbw[:, 12:16], ALU.add).then_inc(lb_own, 1)
            dve.wait_ge(lb_own, 2)
            v.reciprocal(lbw[:, 20:24], lbw[:, 16:20]).then_inc(lb_own, 1)
            dve.wait_ge(lb_own, 3)
            v.tensor_tensor(lbw[:, 24:28], lbw[:, 4:8], lbw[:, 20:24], ALU.mult).then_inc(lb_own, 1)
            dve.wait_ge(lb_own, 4)
            v.tensor_scalar(lbw[:, 28:32], lbw[:, 24:28], -1.0, 1.0, ALU.mult, ALU.add).then_inc(lb_own, 1)
            dve.wait_ge(lb_own, 5)

            def halves(a, w, n):
                return a[:, 0:n].rearrange("p (n a w) -> p n a w", a=2, w=w)

            def diff(h, i):
                w = LEVELS[i]
                n = SEQ if w > 2 else T
                if i == 0:
                    dve.wait_ge(kt_tr, 3 * h + 1)
                    dve.wait_ge(g_ready, h + 1)
                if i >= 2:
                    dve.wait_ge(lev_mm, 8 * h + i - 1)
                g, e = halves(G, w, n), halves(EX[i % 2], w, n)
                mid = g[:, :, 0, w - 1:w].to_broadcast([P, n // (2 * w), w])
                v.tensor_tensor(e[:, :, 0, :], mid, g[:, :, 0, :], ALU.subtract)
                v.tensor_tensor(e[:, :, 1, :], g[:, :, 1, :], mid, ALU.subtract).then_inc(diff_ready, 1)

            def decayed(h, i):
                w = LEVELS[i]
                n = SEQ if w > 2 else T
                e, q, k = halves(EX[i % 2], w, n), halves(Q, w, n), halves(K, w, n)
                dve.wait_ge(exp_ready, 11 * h + i + 1)
                v.tensor_tensor(e[:, :, 0, :], e[:, :, 0, :], k[:, :, 0, :], ALU.mult)
                v.tensor_tensor(e[:, :, 1, :], e[:, :, 1, :], q[:, :, 1, :], ALU.mult).then_inc(x_ready, 1)

            def take(h, i):
                dve.wait_ge(lev_mm, 8 * h + i + 1)
                dve.wait_ge(lev_read, 8 * h + i + 1)
                v.memset(pad[:, i:i + 1], 0.0)
                mask = (levmask[:, i, :] if i < 7 else ident[:]).bitcast(I32)
                for b in range(2):
                    last = v.copy_predicated(SC[:, 4 * b:4 * b + 4, :], mask[:, None, :].to_broadcast([P, 4, P]),
                                             banks[6 + b][:].rearrange("p (n t) -> p n t", n=4))
                if i >= 5:
                    last = v.copy_predicated(SC[0:NS, NP, 0:NS], mask[0:NS, 0:NS], banks[5][0:NS, 0:NS])
                last.then_inc(lev_read, 1)

            def turned(h, waited, to, ready):
                for b in range(2):
                    dve.wait_ge(waited, 3 * h + b + 1 + 1)
                    v.tensor_copy(to[:, 4 * b:4 * b + 4, :].rearrange("p n c -> p (n c)"), banks[3 + b][:]).then_inc(ready, 1)
                dve.wait_ge(waited, 3 * h + 3 + 1)
                v.tensor_copy(to[0:NS, NP, :], banks[5][0:NS, P:2 * P]).then_inc(ready, 1)

            with dve.Fori(0, HB) as h:
                dve.wait_ge(o_mm, h + 1)
                v.memset(SC[:], 0.0).then_inc(sc_zero, 1)
                dve.wait_ge(sig_ready, 2 * h + 1)
                v.tensor_scalar(K[:], K[:], lbw[:, bass.ds(h + 28, 1)], None, ALU.mult).then_inc(k_ready, 1)
                dve.wait_ge(f_ready, h + 1)
                v.tensor_tensor_scan(G[:], resets[:], EX[1][:], 0.0, ALU.mult, ALU.add).then_inc(g_ready, 1)
                dve.wait_ge(q_act, h + 1)
                dve.wait_ge(k_ready, h + 1)
                dve.wait_ge(sc_zero, h + 1)
                for i in range(9):
                    if i < 7:
                        diff(h, i)
                    if i == 1:
                        turned(h, vi_tr, VB, vb_ready)
                    if 1 <= i < 8:
                        decayed(h, i - 1)
                    if i >= 2:
                        take(h, i - 2)
                dve.wait_ge(lev_mm, 8 * h + 7)
                for a, b, w in ((0, SEQ, P), (SEQ, T, DQ)):
                    g = G[:, a:b].rearrange("p (n w) -> p n w", w=w)
                    last = v.tensor_tensor(EX[0][:, a:b].rearrange("p (n w) -> p n w", w=w),
                                           g[:, :, w - 1:w].to_broadcast([P, (b - a) // w, w]), g, ALU.subtract)
                last.then_inc(diff_ready, 1)
                dve.wait_ge(exp_ready, 11 * h + 8)
                v.tensor_tensor(EX[1][:], EX[1][:], Q[:], ALU.mult).then_inc(x_ready, 1)
                dve.wait_ge(exp_ready, 11 * h + 9)
                v.tensor_tensor(EX[0][:], EX[0][:], K[:], ALU.mult).then_inc(x_ready, 1)
                take(h, 7)
                turned(h, kt_tr, KT, kt_ready)
                for t in range(NP + 1):
                    rows = P if t < NP else NS
                    dve.wait_ge(v_tr, 3 * h + min(t // 4, 2) + 1)
                    src = banks[VBANK[t // 4]][0:rows, (t % 4) * P:(t % 4) * P + P] if t < NP else banks[5][0:NS, 0:P]
                    v.bn_stats(bst[0:rows, t, :], src).then_inc(v_own, 1)
                dve.wait_ge(v_own, 21 * h + 9)
                v.memset(pad[:, 8:9], 0.0)
                for t in range(NP + 1):
                    rows = P if t < NP else NS
                    last = v.bn_aggr(bmv[0:rows, t, :], bst[0:rows, t, :])
                last.then_inc(v_stat, 1)
                dve.wait_ge(kv_mm, h + 1)
                dve.wait_ge(exp_ready, 11 * h + 10)
                v.tensor_copy(SS[:, 0, :], banks[3][:, 0:P]).then_inc(st_chain, 1)
                for t in range(1, NP):
                    dve.wait_ge(st_chain, 8 * h + t)
                    v.scalar_tensor_tensor(out=SS[:, t, :], in0=SS[:, t - 1, :], scalar=DG[:, 0, t:t + 1],
                                           in1=banks[3 + t // 4][:, (t % 4) * P:(t % 4) * P + P],
                                           op0=ALU.mult, op1=ALU.add).then_inc(st_chain, 1)
                dve.wait_ge(v_std, h + 1)
                v.reciprocal(brs[:], brs[:]).then_inc(v_own, 1)
                dve.wait_ge(v_own, 21 * h + 10)
                for t in range(NP + 1):
                    rows = P if t < NP else NS
                    src = banks[VBANK[t // 4]][0:rows, (t % 4) * P:(t % 4) * P + P] if t < NP else banks[5][0:NS, 0:P]
                    v.tensor_scalar(VT[0:rows, t, :], src, bmv[0:rows, t, 0:1], brs[0:rows, t:t + 1],
                                    ALU.subtract, ALU.mult).then_inc(v_own, 1)
                dve.wait_ge(v_own, 21 * h + 19)
                for part, (r, a, b) in enumerate(((P, 0, NP), (NS, NP, NP + 1))):
                    x = VT[0:r, a:b, :]
                    v.tensor_tensor(x, x, gainA[0:r, bass.ds(h, 1), :].to_broadcast([r, b - a, P]), ALU.mult).then_inc(v_own, 1)
                for part, (r, a, b) in enumerate(((P, 0, NP), (NS, NP, NP + 1))):
                    dve.wait_ge(v_own, 21 * h + 20 + part)
                    x = VT[0:r, a:b, :]
                    v.tensor_tensor(x, x, biasA[0:r, bass.ds(h, 1), :].to_broadcast([r, b - a, P]), ALU.add).then_inc(vt_ready, 1)
                v.tensor_tensor(VX, VB[0:NS, NP:NP + 1, :].to_broadcast([NS, DEC, P]),
                                sel[:, :, None].to_broadcast([NS, DEC, P]), ALU.mult).then_inc(vx_ready, 1)
                dve.wait_ge(sv_mm, h + 1)
                dve.wait_ge(u_act, h + 1)
                for b, c, o in ((6, slice(0, 512), 0), (7, slice(512, SEQ), 0), (5, slice(SEQ, T), 256)):
                    n = c.stop - c.start
                    last = v.tensor_tensor(R[:, bass.ds(h, 1), c].rearrange("p k t -> p (k t)"), U[:, c],
                                           banks[b][:, o:o + n], ALU.mult)
                last.then_inc(a_done, 1)
                dve.wait_ge(o_mm, h + 1 + 1)
                dve.wait_ge(exp_ready, 11 * h + 11)
                v.tensor_tensor(S0[:], S0[:], DG[:, 1, :, None].to_broadcast([P, DEC, P]), ALU.mult).then_inc(sst_own, 1)
                dve.wait_ge(sst_own, 3 * h + 1)
                dve.wait_ge(skv_mm, h + 1)
                for b in range(2):
                    s4 = S0[:, 4 * b:4 * b + 4, :].rearrange("p n v -> p (n v)")
                    v.tensor_tensor(s4, s4, banks[3 + b][:], ALU.add).then_inc(sst_own, 1)
                dve.wait_ge(rms_std, 3 * h + 3 + 1)
                v.reciprocal(Q[:], Q[:]).then_inc(o_own, 1)
                dve.wait_ge(o_own, 2 * h + 1)
                v.scalar_tensor_tensor(out=K[:], in0=K[:], scalar=lbp[:, 12:13], in1=Q[:], op0=ALU.mult,
                                       op1=ALU.mult).then_inc(o_own, 1)
                dve.wait_ge(o_own, 2 * h + 2)
                dve.wait_ge(sg_act, h + 1)
                v.tensor_tensor(R[:, bass.ds(h + HB, 1), :].rearrange("p k t -> p (k t)"), K[:], SGG[:],
                                ALU.mult).then_inc(b_done, 1)

            for k in range(KD):
                dve.wait_ge(m_hi, k + 1)
                v.tensor_tensor(HL[:, k, :], R[:, k, :], HH[:, k, :].bitcast(F32), ALU.subtract).then_inc(m_lo, 1)

            def attention_dve():
                dve.wait_ge(at_pool, 8)
                with dve.Fori(0, NPAIR) as hp:
                    def pages_copied(gs):
                        for g in gs:
                            dve.wait_ge(kp_tr, 16 * hp + g + 3 + 1)
                            if g >= 2:
                                dve.wait_ge(kp_z, 16 * hp + g - 1)
                            v.tensor_copy(KTP[g % 2][:], banks[3 + g % 2][:]).then_inc(kp_ev, 1)

                    for c in range(3):
                        dve.wait_ge(q_hi, 3 * hp + c + 1)
                        v.scalar_tensor_tensor(out=QL[:, CH[c]], in0=banks[c][:, 0:CW], scalar=0.125,
                                               in1=QH[:, CH[c]].bitcast(F32), op0=ALU.mult, op1=ALU.subtract).then_inc(qk_free, 1)
                    for c in range(3):
                        dve.wait_ge(k_hi, 3 * hp + c + 1)
                        v.tensor_tensor(KL[:, CH[c]], banks[c][:, 0:CW], KH[:, CH[c]].bitcast(F32), ALU.subtract).then_inc(qk_free, 1)
                        pages_copied(GROUPS_AT[c])
                    for c in range(3, 6):
                        pages_copied(GROUPS_AT[c])
                    dve.wait_ge(kv_store, 64 * hp + 16)
                    for b in range(2):
                        dve.wait_ge(ktok_tr, 3 * hp + b + 1)
                        v.tensor_copy(KTOK[:, 4 * b:4 * b + 4, :].rearrange("p n c -> p (n c)"), banks[b][:]).then_inc(ktok_ev, 1)
                    dve.wait_ge(ktok_tr, 3 * hp + 3)
                    v.tensor_copy(KTOK[0:NS, NP, :], banks[2][0:NS, 0:P]).then_inc(ktok_ev, 1)
                    def sample_part(s):
                        if s == -2:
                            dve.wait_ge(nz_ready, 2 * hp + 2)
                            v.tensor_tensor(NZ[:], NZ[:], capnew[:], ALU.min).then_inc(nz_own, 1)
                            dve.wait_ge(nz_own, hp + 1)
                            v.tensor_scalar(NE[:], NZ[:], ZCAP, None, ALU.min).then_inc(ne_min, 1)
                            dve.wait_ge(dz_ready, 2 * hp + 2)
                            v.tensor_scalar(DE[:], DZ[:], ZCAP, None, ALU.min).then_inc(de_min, 1)
                        if s == 0:
                            dve.wait_ge(ne_act, 2 * hp + 2)
                            v.tensor_tensor(NE[:], NE[:], NZ[:], ALU.max).then_inc(nsp_ready, 1)
                            v.memset(DSUF[:, :, PAGES - 1, :], 0.0).then_inc(dsuf, 1)
                        if s == 1:
                            dve.wait_ge(nsp_ready, hp + 1)
                            dve.wait_ge(dsuf, 9 * hp + 1)
                            v.tensor_copy(DSUF[0:NS, :, PAGES - 1, :], NE[:].rearrange("p n h i -> p n (h i)")).then_inc(dsuf, 1)
                            dve.wait_ge(de_act, 2 * hp + 2)
                            v.tensor_tensor(DE[:], DE[:], DZ[:], ALU.max).then_inc(dsp_ready, 1)
                        if s == 2:
                            dve.wait_ge(dsp_ready, hp + 1)
                        if 2 <= s <= 5:
                            for g in range(PAGES - 2 - 2 * (s - 2), max(PAGES - 4 - 2 * (s - 2), -1), -1):
                                dve.wait_ge(dsuf, 9 * hp + PAGES - g)
                                v.tensor_tensor(DSUF[:, :, g, :], DSUF[:, :, g + 1, :], DE[:, :, g + 1, :, :].rearrange("p n h i -> p n (h i)"),
                                                ALU.add).then_inc(dsuf, 1)
                        if s == 7:
                            dve.wait_ge(rn_mm, hp + 1)
                            v.tensor_tensor(NZ[:].rearrange("p n h i -> p (n h i)"), NZ[:].rearrange("p n h i -> p (n h i)"),
                                            banks[0][0:NS, 0:64], ALU.subtract).then_inc(narg, 1)
                            dve.wait_ge(rd_mm, hp + 1)
                            v.tensor_tensor(DZ[:].rearrange("p n g h i -> p (n g h i)"), DZ[:].rearrange("p n g h i -> p (n g h i)"),
                                            banks[5][:], ALU.subtract).then_inc(darg, 1)

                    def softplus_in(s):
                        c = slice(LOW[s], 512)
                        z, e = Z[s % 4], E[s % 2]
                        dve.wait_ge(zc, NST * hp + s + 1)
                        if DIAG[s]:
                            d = z[:, LOW[s]:LOW[s] + P]
                            v.tensor_tensor(d, d, cap[:], ALU.min).then_inc(capped, 1)
                            dve.wait_ge(capped, sum(DIAG) * hp + sum(DIAG[:s + 1]))
                        if s >= 2:
                            dve.wait_ge(spl_ready, NST * hp + s - 1)
                        v.tensor_scalar(e[:, c], z[:, c], ZCAP, None, ALU.min).then_inc(e_min, 1)

                    def softplus_out(s):
                        c = slice(LOW[s], 512)
                        dve.wait_ge(e_ln, NST * hp + s + 1)
                        v.tensor_tensor(E[s % 2][:, c], E[s % 2][:, c], Z[s % 4][:, c], ALU.max).then_inc(sp_ready, 1)
                        dve.wait_ge(sp_ready, NST * hp + s + 1)
                        if s >= 2:
                            if FINAL[s - 2]:
                                dve.wait_ge(tri_mm, NST * hp + s - 1)
                            else:
                                dve.wait_ge(carry_mm, NCARRY * hp + carries(s - 2))
                        v.tensor_copy(SPH[s % 2][:, c], E[s % 2][:, c]).then_inc(sph_ready, 1)

                    def exponent(s):
                        z = Z[s % 4][:, LOW[s]:512]
                        dve.wait_ge(tri_mm, NST * hp + s + 1)
                        v.tensor_tensor(z, z, banks[3][:, LOW[s]:512], ALU.subtract).then_inc(arg_ready, 1)

                    for s in range(-2, NST):
                        if s + 2 < NST:
                            softplus_in(s + 2)
                        if s >= 0:
                            exponent(s)
                        if s + 2 < NST:
                            softplus_out(s + 2)
                        sample_part(s)
                for k in range(KD):
                    dve.wait_ge(m_hi, KD + k + 1)
                    v.tensor_tensor(HL[:, k, :], R[:, k, :], HH[:, k, :].bitcast(F32), ALU.subtract).then_inc(m_lo, 1)

            def residual(stage, g):
                with dve.Fori(0, KD // 2) as j:
                    for s in range(2):
                        for c in range(3):
                            u = 6 * j + 3 * s + c
                            r, xh, xl = (a[:, bass.ds(2 * j + s, 1), CH[c]].rearrange("p k t -> p (k t)") for a in (R, XH, XL))
                            dve.wait_ge(d_mm, 3 * TB[stage] + u + 4 + 1)
                            if g:
                                v.tensor_tensor(r, r, banks[c][:, 0:CW], ALU.add).then_inc(res1, 1)
                                continue
                            v.scalar_tensor_tensor(out=r, in0=xh.bitcast(F32), scalar=ALPHA, in1=banks[c][:, 0:CW],
                                                   op0=ALU.mult, op1=ALU.add).then_inc(res1, 1)
                            dve.wait_ge(res1, units[stage] + u + 4)
                            v.scalar_tensor_tensor(out=r, in0=xl.bitcast(F32), scalar=ALPHA, in1=r,
                                                   op0=ALU.mult, op1=ALU.add).then_inc(res, 1)

            def bcast(a, c):
                return a[:, None, CH[c]].to_broadcast([P, KD, CW])

            def norm_dve(n):
                dve.wait_ge(res1, ln_units[n][0] + 3)
                dve.wait_ge(res, ln_units[n][1])
                for c in range(3):
                    v.tensor_reduce(LS[:, CH[c]], R[:, :, CH[c]].rearrange("p k t -> p t k"), AX, ALU.add).then_inc(ln_sum, 1)
                for c in range(3):
                    dve.wait_ge(ln_mean, 3 * n + c + 1)
                    v.scalar_tensor_tensor(out=R[:, :, CH[c]], in0=banks[3 + c][:, None, 0:CW].to_broadcast([P, KD, CW]),
                                           scalar=-1.0 / D, in1=R[:, :, CH[c]], op0=ALU.mult, op1=ALU.add).then_inc(ln_cent, 1)
                for c in range(3):
                    dve.wait_ge(ln_sq, 3 * n + c + 1)
                    v.tensor_reduce(LS[:, CH[c]], SQ[c % 2][:].rearrange("p k t -> p t k"), AX, ALU.add).then_inc(ln_sum2, 1)
                for c in range(3):
                    dve.wait_ge(ln_std, 3 * n + c + 1)
                    v.reciprocal(RS[:, CH[c]], RS[:, CH[c]]).then_inc(ln_rstd, 1)
                    dve.wait_ge(ln_rstd, 3 * n + c + 1)
                    v.tensor_tensor(R[:, :, CH[c]], R[:, :, CH[c]], bcast(RS, c), ALU.mult).then_inc(ln_norm, 1)

            for l in range(LAYERS):
                if l == 1:
                    attention_dve()
                residual(("about", "cout")[l], 0)
                norm_dve(2 * l)
                for g, (_, kg) in enumerate(GROUPS):
                    done = ffn_pairs[l, g]
                    with dve.Fori(0, kg) as j:
                        for c in range(3):
                            dve.wait_ge(gate_read, 3 * done + 3 * j + c + 1)
                            dve.wait_ge(d_mm, 3 * TB["up", l, g] + 6 * j + 3 + c + 4 + 1)
                            dve.wait_ge(h_lo, 3 * done + 3 * j + c + 1)
                            v.tensor_tensor(HF[c][:], SG[c][:], banks[c][:, 0:CW], ALU.mult).then_inc(up_read, 1)
                        for c in range(3):
                            hh, hl = (a[:, bass.ds(j, 1), CH[c]].rearrange("p k t -> p (k t)") for a in (HH, HL))
                            dve.wait_ge(h_hi, 3 * done + 3 * j + c + 1)
                            v.tensor_tensor(hl, HF[c][:], hh.bitcast(F32), ALU.subtract).then_inc(h_lo, 1)
                    residual(("down", l, g), g)
                norm_dve(2 * l + 1)
            for n in range(NP + 1):
                rows = P if n < NP else NS
                for b in range(2):
                    dve.wait_ge(y_tr, 2 * n + b + 1)
                    if n >= 2:
                        dve.wait_ge(y_out[n % 2], 16 * (n // 2))
                    v.tensor_copy(YT[n % 2][0:rows, 512 * b:512 * b + 512], banks[2 * (n % 2) + b][0:rows, :]).then_inc(y_ev, 1)

        @block.tensor
        def _(pe):
            t = nc.tensor
            pe.wait_ge(set_pool, 7)
            pe.wait_ge(set_dve, 1)
            pe.wait_ge(par_load, 16 * 11)
            t.transpose(banks[6][:, 0:64], PROWS, ident[0:64, 0:64]).then_inc(par_mm, 1)
            t.transpose(banks[6][:, 64:77], LROWS, ident[0:13, 0:13]).then_inc(par_mm, 1)
            t.matmul(banks[6][:, 128:144], ones[0:1, :], BROW[:, 1024:1040], start=True, stop=True).then_inc(par_mm, 1)
            for h in range(HB):
                last = t.transpose(banks[7][:, h * P:(h + 1) * P], KT[:, h, :], ident[:])
            last.then_inc(par_mm, 2)
            for k in range(KD):
                if k >= 2:
                    pe.wait_ge(xt_lo, k - 1)
                if k == 0:
                    pe.wait_ge(x_load, 16 * (NP + 1))
                for n in range(NP):
                    t.transpose(banks[3 * (k % 2) + n // 4][:, (n % 4) * P:(n % 4) * P + P], XP[:, n, k * P:(k + 1) * P], ident[:])
                t.transpose(banks[3 * (k % 2) + 2][:, 0:NS], XS[:, k * P:(k + 1) * P], ident[0:NS, 0:NS]).then_inc(xt_mm, 1)
            pe.wait_ge(par_ev, 5)
            for i in range(2):
                t.matmul(banks[6 + i][:], ones[0:1, :], BROW[:, 512 * i:512 * i + 512], start=True, stop=True).then_inc(par_mm, 1)
            pe.wait_ge(xt_lo, KD)
            pe.wait_ge(par_ev, 8)
            pe.wait_ge(lb_own, 5)
            pe.wait_ge(ws_load, 16 * DEC)
            pe.wait_ge(wt_done, 1)

            def product(slot, kb, c, xh, xl):
                n = 0
                for k in range(kb):
                    for w, x in ((WH, xh), (WL, xh), (WH, xl)):
                        last = t.matmul(banks[c][:, 0:CW], w[slot][:, k, :], x[:, k, CH[c]],
                                        start=n == 0, stop=n == 3 * kb - 1)
                        n += 1
                return last.then_inc(d_mm, 1)

            def scores(h, i):
                if i < 7:
                    pe.wait_ge(x_ready, 9 * h + i + 1)
                pe.wait_ge(lev_read, 8 * h + i + 1)
                left, right = (K, Q) if i == 7 else (EX[i % 2], EX[i % 2])
                for n in range(NP):
                    c = slice(n * P, (n + 1) * P)
                    last = t.matmul(banks[6 + n // 4][:, (n % 4) * P:(n % 4) * P + P], left[:, c], right[:, c], start=True, stop=True)
                if i >= 5:
                    last = t.matmul(banks[5][0:NS, 0:NS], left[:, SEQ:T], right[:, SEQ:T], start=True, stop=True)
                last.then_inc(lev_mm, 1)

            def turn(src, b0, b2, o2, done):
                for n in range(NP):
                    last = t.transpose(banks[b0 + n // 4][:, (n % 4) * P:(n % 4) * P + P], src[:, n * P:(n + 1) * P], ident[:])
                    if n % 4 == 3:
                        last.then_inc(done, 1)
                t.transpose(banks[b2][0:NS, o2:o2 + P], src[:, SEQ:T], ident[:]).then_inc(done, 1)

            with pe.Fori(0, HB) as h:
                n = 18 * h
                for j in range(6):
                    for c in range(3):
                        if c == 0:
                            pe.wait_ge(w_split, 12 * h + 2 * j + 4 + 1)
                        pe.wait_ge(d_ev, n + 3 * j + c + 1)
                        product(j % 2, KD, c, XH, XL)
                        if 9 <= 3 * j + c < 17:
                            scores(h, 3 * j + c - 9)
                    if j == 2:
                        pe.wait_ge(d_ev, n + 12)
                        pe.wait_ge(rms_std, 3 * h + 1)
                        turn(U, 3, 5, P, vi_tr)
                pe.wait_ge(x_ready, 9 * h + 9)
                pe.wait_ge(vb_ready, 3 * h + 3)
                pe.wait_ge(lev_read, 8 * h + 9)
                turn(EX[0], 3, 5, P, kt_tr)
                pe.wait_ge(kt_ready, 3 * h + 3)
                pe.wait_ge(v_act, h + 1)
                turn(V, 6, 5, 0, v_tr)
                for m in range(NP):
                    last = t.matmul(banks[3 + m // 4][:, (m % 4) * P:(m % 4) * P + P], KT[:, m, :], VB[:, m, :], start=True, stop=True)
                last.then_inc(kv_mm, 1)
                pe.wait_ge(vt_ready, 2 * h + 2)
                for m in range(NP):
                    to = banks[6 + m // 4][:, (m % 4) * P:(m % 4) * P + P]
                    t.matmul(to, VT[:, m, :], WT[:, bass.ds(h, 1), :].rearrange("p h t -> p (h t)"), start=True, stop=False)
                    t.matmul(to, ones[0:1, :], bsrow[:, bass.ds(h, 1), :].rearrange("p h t -> p (h t)"), start=False, stop=True)
                to = banks[5][:, 256:256 + NS]
                t.matmul(to, VT[0:NS, NP, :], WS[:, bass.ds(h, 1), :].rearrange("p h t -> p (h t)"), start=True, stop=False)
                t.matmul(to, ones[0:1, :], bsS[:, bass.ds(h, 1), :, :].rearrange("p h n t -> p (h n t)"),
                         start=False, stop=True).then_inc(sv_mm, 1)
                pe.wait_ge(vx_ready, h + 1)
                pe.wait_ge(st_chain, 8 * h + 8)
                for b in range(2):
                    last = t.matmul(banks[3 + b][:], KT[0:NS, NP, :], VX[:, 4 * b:4 * b + 4, :].rearrange("p n v -> p (n v)"),
                                    start=True, stop=True)
                last.then_inc(skv_mm, 1)
                pe.wait_ge(a_done, h + 1)
                pe.wait_ge(s0_load, 16 * h + 16)
                for m in range(NP):
                    to = banks[6 + m // 4][:, (m % 4) * P:(m % 4) * P + P]
                    t.matmul(to, VB[:, m, :], SC[:, m, :], start=True, stop=m == 0)
                    if m:
                        t.matmul(to, SS[:, m - 1, :], EX[1][:, m * P:(m + 1) * P], start=False, stop=True)
                t.matmul(banks[5][:, 0:NS], VB[0:NS, NP, :], SC[0:NS, NP, 0:NS], start=True, stop=False, skip_group_check=True)
                for m in range(DEC):
                    last = t.matmul(banks[5][:, DQ * m:DQ * m + DQ], S0[:, m, :], EX[1][:, SEQ + DQ * m:SEQ + DQ * m + DQ],
                                    start=False, stop=True, skip_group_check=True)
                last.then_inc(o_mm, 1)
                pe.wait_ge(osq, h + 1)
                pe.wait_ge(sst_own, 3 * h + 3)
                for c in range(3):
                    last = t.matmul(banks[3 + c][:, 0:CW], ones[:], G[:, CH[c]], start=True, stop=True)
                last.then_inc(ms_mm, 1)

            def attention_pe():
                n0 = TB["c"]
                pe.wait_ge(res1, units["down", 0, 2] + 3 * KD + 3)
                pe.wait_ge(ln_std, 6)
                pe.wait_ge(ln_cent, 6)
                pe.wait_ge(at_pool, 8)
                with pe.Fori(0, NPAIR) as hp:
                    n = n0 + 3 * hp

                    def turn_pages(g):
                        if g % 2 == 0:
                            pe.wait_ge(kp_load[g // 2 % 2], 16 * PAGES * (4 * hp + g // 4 + 1))
                        if g >= 2:
                            pe.wait_ge(kp_ev, 16 * hp + g - 1)
                        for i in range(4):
                            last = t.transpose(banks[3 + g % 2][:, i * P:(i + 1) * P], KP[g // 2 % 2][:, 4 * (g % 2) + i, :], ident[:])
                        last.then_inc(kp_tr, 1)

                    def page_logits(g):
                        pe.wait_ge(kp_ev, 16 * hp + g + 1)
                        if g == 0:
                            pe.wait_ge(q_hi, 3 * hp + 3)
                            pe.wait_ge(do_ev, 2 * hp + 1)
                        for i in range(4):
                            o = 64 * (g // 2) + 8 * (4 * (g % 2) + i)
                            last = t.matmul(banks[5][:, o:o + 8], KTP[g % 2][:, i * P:(i + 1) * P],
                                            QD[:, g // 2].rearrange("p h i -> p (h i)"), start=True, stop=True)
                        last.then_inc(kp_z, 1)

                    for j in range(3):
                        for c in range(3):
                            if c == 0:
                                pe.wait_ge(w_split, 2 * n + 2 * j + 4 + 1)
                            if j == 0:
                                pe.wait_ge(x_lo, 3 + c + 1)
                                pe.wait_ge(v_free, 3 * hp + c + 1)
                                if c == 0:
                                    pe.wait_ge(narg, hp + 1)
                            else:
                                pe.wait_ge(qk_free, 6 * hp + 3 * (j - 1) + c + 1)
                            product(j % 2, KD, c, XH, XL)
                            if j:
                                if j == 1 and c == 0:
                                    pe.wait_ge(po_ev, 4 * hp + 1)
                                for g in GROUPS_AT[3 * (j - 1) + c]:
                                    turn_pages(g)
                                    if g:
                                        page_logits(g - 1)
                    page_logits(15)
                    pe.wait_ge(v_free, 3 * hp + 6)
                    for src, bs, done in ((KF, (0, 1, 2), ktok_tr), (VI, (6, 7, 3), vtok_tr)):
                        for m in range(NP):
                            last = t.transpose(banks[bs[m // 4]][:, (m % 4) * P:(m % 4) * P + P], src[:, m * P:(m + 1) * P], ident[:])
                            if m % 4 == 3:
                                last.then_inc(done, 1)
                        t.transpose(banks[bs[2]][0:NS, 0:P], src[:, SEQ:T], ident[:]).then_inc(done, 1)
                    t.matmul(banks[4][0:NS, 0:64], KF[:, SEQ:T], QD[:].rearrange("p n h i -> p (n h i)"), start=True, stop=True).then_inc(zn_mm, 1)

                    def logits(s):
                        h, c, b = STEPS[s]
                        r, lo = slice(64 * h, 64 * h + 64), LOW[s]
                        if s < 2:
                            pe.wait_ge(vtok_ev, 3 * hp + 3)
                            pe.wait_ge(qk_free, 6 * hp + 6)
                        else:
                            pe.wait_ge(zc, NST * hp + s - 1)
                        for i, (k, q) in enumerate(((KH, QH), (KL, QH), (KH, QL))):
                            last = t.matmul(banks[6 + s % 2][:, lo:512], k[r, b * P:(b + 1) * P], q[r, 512 * c + lo:512 * c + 512],
                                            start=i == 0, stop=i == 2)
                        last.then_inc(z_mm, 1)

                    def sums(s, m, first, done):
                        lo = LOW[s]
                        t.matmul(banks[3][:, lo:512], m[:], SPH[s % 2][:, lo:512], start=first, stop=False, skip_group_check=True)
                        t.matmul(banks[3][:, lo:512], m[:], SPL[s % 2][:, lo:512], start=False, stop=True,
                                 skip_group_check=True).then_inc(done, 1)

                    def values(s):
                        h, c, b = STEPS[s]
                        r, lo = slice(64 * h, 64 * h + 64), LOW[s]
                        pe.wait_ge(w_ready, NST * hp + s + 1)
                        if FIRST[s]:
                            pe.wait_ge(po_ev, 4 * hp + chunks_done(s) + 1)
                            pe.wait_ge(nz_ready, 2 * hp + 2)
                        t.matmul(banks[4][r, lo:512], VTOK[:, b, r], Z[s % 4][:, lo:512], start=FIRST[s], stop=FINAL[s],
                                 skip_group_check=True).then_inc(pv_mm, 1)

                    def sample_values(m):
                        if m == 0:
                            pe.wait_ge(dw_ready, hp + 1)
                            pe.wait_ge(nw_ready, hp + 1)
                        pe.wait_ge(vp_load[m % 2], 16 * PAGES * (4 * hp + m // 2 + 1))
                        to = banks[5][:, 8 * m:8 * m + 8]
                        for g in range(PAGES):
                            t.matmul(to, VP[m % 2][:, g, :], DE[:, m, g].rearrange("p h i -> p (h i)"), start=g == 0, stop=False)
                        t.matmul(to, VTOK[0:NS, NP, :], NE[:, m].rearrange("p h i -> p (h i)"), start=False, stop=True).then_inc(dv_mm, 1)

                    for s in range(3):
                        logits(s)
                    pe.wait_ge(ktok_ev, 3 * hp + 3)
                    for s in range(NST):
                        pe.wait_ge(spl_ready, NST * hp + s + 1)
                        if FIRST[s] and s:
                            pe.wait_ge(arg_ready, NST * hp + s)
                        sums(s, triR, FIRST[s], tri_mm)
                        if s:
                            values(s - 1)
                        if s + 3 < NST:
                            logits(s + 3)
                        if s == 6:
                            pe.wait_ge(nsp_ready, hp + 1)
                            t.matmul(banks[0][:, 0:64], tri[0:NS, :], NE[:].rearrange("p n h i -> p (n h i)"), start=True,
                                     stop=True).then_inc(rn_mm, 1)
                            pe.wait_ge(dsuf, 9 * hp + 9)
                            pe.wait_ge(dz_ready, 2 * hp + 2)
                            t.matmul(banks[5][:], tri[:], DE[:].rearrange("p n g h i -> p (n g h i)"), start=True, stop=False)
                            t.matmul(banks[5][:], ones[:], DSUF[:].rearrange("p n g i -> p (n g i)"), start=False, stop=True).then_inc(rd_mm, 1)
                        if s >= 9 and s % 2:
                            sample_values((s - 9) // 2)
                        if not FINAL[s]:
                            pe.wait_ge(arg_ready, NST * hp + s + 1)
                            sums(s, restR, False, carry_mm)
                    values(NST - 1)
                pe.wait_ge(m_lo, 2 * KD)

            def out_stage(stage, kb):
                with pe.Fori(0, KD // 2) as j:
                    for s in range(2):
                        for c in range(3):
                            if c == 0:
                                pe.wait_ge(w_split, 2 * TB[stage] + 4 * j + 2 * s + 4 + 1)
                            pe.wait_ge(res1, units[stage] + 6 * j + 3 * s + c + 1)
                            product(s, kb, c, HH, HL)

            def norm_pe(n):
                for c in range(3):
                    pe.wait_ge(ln_sum, 3 * n + c + 1)
                    t.matmul(banks[3 + c][:, 0:CW], ones[:], LS[:, CH[c]], start=True, stop=True).then_inc(ln_mean, 1)
                for c in range(3):
                    pe.wait_ge(ln_sum2, 3 * n + c + 1)
                    if c == 2:
                        pe.wait_ge(ln_cent, 3 * n + 1)
                    t.matmul(banks[VARB[c]][:, 0:CW], ones[:], LS[:, CH[c]], start=True, stop=True).then_inc(ln_var, 1)

            pe.wait_ge(m_lo, KD)
            for l in range(LAYERS):
                if l == 1:
                    attention_pe()
                out_stage(("about", "cout")[l], KD)
                norm_pe(2 * l)
                for g, (_, kg) in enumerate(GROUPS):
                    stage, done = ("up", l, g), ffn_pairs[l, g]
                    if g:
                        pe.wait_ge(res1, units["down", l, g - 1] + 3 * KD + 3)
                    with pe.Fori(0, kg) as j:
                        for s in range(2):
                            for c in range(3):
                                if c == 0:
                                    pe.wait_ge(w_split, 2 * TB[stage] + 4 * j + 2 * s + 4 + 1)
                                if s == 0:
                                    pe.wait_ge(x_lo, 6 * l + c + 1)
                                    pe.wait_ge(up_read, 3 * done + 3 * j + c + 1)
                                else:
                                    pe.wait_ge(gate_read, 3 * done + 3 * j + c + 1)
                                product(s, KD, c, XH, XL)
                    pe.wait_ge(h_lo, 3 * (done + kg) + 3)
                    out_stage(("down", l, g), kg)
                norm_pe(2 * l + 1)
            for n in range(NP + 1):
                rows = P if n < NP else NS
                if n == 0:
                    pe.wait_ge(ln_aff, 24 * LAST_LN + 24)
                if n >= 2:
                    pe.wait_ge(y_ev, 2 * n - 2)
                for k in range(KD):
                    last = t.transpose(banks[2 * (n % 2) + k // 4][0:rows, (k % 4) * P:(k % 4) * P + P],
                                       R[:, k, n * P:n * P + rows], ident[:])
                    if k % 4 == 3:
                        last.then_inc(y_tr, 1)


_INS = ["x_prompt", "x_sample", "state_b", "cache_k", "cache_v", "page_table", "ab_w_in", "ab_w_out", "a_w_s",
        "a_b_s", "a_ln_g", "a_ln_b", "b_lb_logits", "b_norm_g", "c_w_in", "c_w_out", "c_logit_bias", "ln1_g",
        "ln1_b", "ln2_g", "ln2_b", "ffn_w_gate", "ffn_w_up", "ffn_w_down"]
_OUTS = [(1, SEQ, D), (DEC, DQ, D), (1, DEC, DQ, 512), (1, 1, HB, P, P), (1, DEC, HB, P, P),
         (1, 1, SEQ, 16, 64), (1, 1, SEQ, 16, 64), (1, DEC, DQ, 16, 64), (1, DEC, DQ, 16, 64)]


def kernel(**inputs):
    import numpy as _np
    import concourse.bacc as _bacc
    from concourse import mybir as _mybir
    from concourse.bass_utils import run_bass_kernel_spmd as _run

    nc = _bacc.Bacc("TRN2", target_bir_lowering=False, num_devices=1)
    arrays, args = {}, []
    for name in _INS:
        a = _np.ascontiguousarray(inputs[name])
        arrays[f"in_{name}_dram"] = a
        args.append(nc.dram_tensor(f"in_{name}_dram", a.shape, _mybir.dt.from_np(a.dtype), kind="ExternalInput").ap())
    for i, shape in enumerate(_OUTS):
        args.append(nc.dram_tensor(f"out_{i}_dram", shape, _mybir.dt.float32, kind="ExternalOutput").ap())
    hybrid_step(nc, *args)
    r = _run(nc, [arrays], core_ids=[0])
    return tuple(r.results[0][f"out_{i}_dram"] for i in range(len(_OUTS)))
```

```python
from contextlib import ExitStack

import concourse.bass as bass
from concourse import mybir

F32 = mybir.dt.float32
F32R = mybir.dt.float32r
I32 = mybir.dt.int32
ALU = mybir.AluOpType
ACT = mybir.ActivationFunctionType
AX = mybir.AxisListType.X

P = 128
D = 1024
KD = D // P
SEQ = 1024
DEC = 8
DQ = 4
NS = DEC * DQ
T = SEQ + NS
NP = SEQ // P
CW = T // 3
CH = [slice(c * CW, (c + 1) * CW) for c in range(3)]
HB = 4
FFN = 2816
NF = FFN // P
GROUPS = [(0, 8), (8, 8), (16, 6)]
PAGES = 8
NPAIR = 8
LEVELS = [64, 32, 16, 8, 4, 2, 1]
LAYERS = 2
ALPHA = (2 * LAYERS) ** 0.25
LN_EPS = 1e-5
RMS_EPS = 1e-6
MASKED = -30000.0
ZCAP = 40.0

AB_TILES = 6 * HB
TB = {"ab": 0, "about": AB_TILES}
_n = AB_TILES + KD
for _l in range(LAYERS):
    if _l == 1:
        TB["c"] = _n
        _n += 3 * NPAIR
        TB["cout"] = _n
        _n += KD
    for _g, (_b, _k) in enumerate(GROUPS):
        TB["up", _l, _g] = _n
        _n += 2 * _k
        TB["down", _l, _g] = _n
        _n += KD
N_TILES = _n
SLOT_LOADS = {}
for _s, _t in TB.items():
    late = _t > TB["c"]
    SLOT_LOADS[_s] = (_t // 2 + (NPAIR // 2 if late else 0), _t // 2 - (NPAIR // 2 if late else 0))


def hybrid_step(nc, x_prompt, x_sample, state_b, cache_k, cache_v, page_table, ab_w_in, ab_w_out, a_w_s, a_b_s,
                a_ln_g, a_ln_b, b_lb_logits, b_norm_g, c_w_in, c_w_out, c_logit_bias, ln1_g, ln1_b, ln2_g, ln2_b,
                ffn_w_gate, ffn_w_up, ffn_w_down, y_prompt, y_sample, a_v_sample, state_b_prompt, state_b_sample,
                ck_prompt, cv_prompt, ck_sample, cv_sample):
    ctx = ExitStack()
    with ctx:
        def sem(name):
            return ctx.enter_context(nc.semaphore(name))

        def place(stack, name, shape, dt=F32):
            return stack.enter_context(nc.sbuf_tensor(name, shape, dt))

        XH = place(ctx, "XH", [P, KD, T], F32R)
        XL = place(ctx, "XL", [P, KD, T], F32R)
        R = place(ctx, "R", [P, KD, T])
        RAW = [place(ctx, f"RAW{s}", [P, KD, P]) for s in range(2)]
        WH = [place(ctx, f"WH{s}", [P, KD, P], F32R) for s in range(2)]
        WL = [place(ctx, f"WL{s}", [P, KD, P], F32R) for s in range(2)]
        ident = place(ctx, "ident", [P, P])
        ones = place(ctx, "ones", [P, P])
        tri = place(ctx, "tri", [P, P])
        triR = place(ctx, "triR", [P, P], F32R)
        restR = place(ctx, "restR", [P, P], F32R)
        zero = place(ctx, "zero", [P, 1])
        epsln = place(ctx, "epsln", [P, 1])
        epsrms = place(ctx, "epsrms", [P, 1])
        lnp = place(ctx, "lnp", [P, 4, 2, KD])
        lbp = place(ctx, "lbp", [P, 16])
        lbw = place(ctx, "lbw", [P, 40])
        cbias = place(ctx, "cbias", [P, 16])

        with ExitStack() as s:
            levmask = place(s, "levmask", [P, 7, P])
            resets = place(s, "resets", [P, T])
            credit = place(s, "credit", [P, 24])
            pad = place(s, "pad", [P, 9])
            sel = place(s, "sel", [NS, DEC])
            WT = place(s, "WT", [P, HB, P])
            WS = place(s, "WS", [NS, HB, NS])
            bsrow = place(s, "bsrow", [1, HB, P])
            bsS = place(s, "bsS", [1, HB, DEC, DQ])
            gainA = place(s, "gainA", [P, HB, P])
            biasA = place(s, "biasA", [P, HB, P])
            U = place(s, "U", [P, T])
            V = place(s, "V", [P, T])
            VT = place(s, "VT", [P, NP + 1, P])
            Q = place(s, "Q", [P, T])
            K = place(s, "K", [P, T])
            G = place(s, "G", [P, T])
            EX = [place(s, f"EX{i}", [P, T]) for i in range(2)]
            VB = place(s, "VB", [P, NP + 1, P])
            SGG = place(s, "SGG", [P, T])
            SC = place(s, "SC", [P, NP + 1, P])
            KT = place(s, "KT", [P, NP + 1, P])
            SS = place(s, "SS", [P, NP, P])
            S0 = place(s, "S0", [P, DEC, P])
            DG = place(s, "DG", [P, 2, 8])
            bst = place(s, "bst", [P, NP + 1, 6])
            bmv = place(s, "bmv", [P, NP + 1, 2])
            brs = place(s, "brs", [P, NP + 1])
        VX = V[0:NS, 0:DEC * P].rearrange("p (n v) -> p n v", n=DEC)
        XS = U[0:NS, 0:D]
        with ExitStack() as s:
            QH, QL, KH, KL = (place(s, n, [P, T], F32R) for n in ("QH", "QL", "KH", "KL"))
            KF = place(s, "KF", [P, T])
            VI = place(s, "VI", [P, T])
            KTOK = place(s, "KTOK", [P, NP + 1, P])
            VTOK = place(s, "VTOK", [P, NP + 1, P])
            Z = [place(s, f"Z{i}", [P, 512]) for i in range(4)]
            E = [place(s, f"E{i}", [P, 512]) for i in range(2)]
            SPH = [place(s, f"SPH{i}", [P, 512], F32R) for i in range(2)]
            SPL = [place(s, f"SPL{i}", [P, 512], F32R) for i in range(2)]
            PG = [place(s, f"PG{i}", [P, PAGES, P]) for i in range(4)]
            KTP = [place(s, f"KTP{i}", [P, 512]) for i in range(2)]
            DZ = place(s, "DZ", [P, DEC, PAGES, 2, DQ])
            DE = place(s, "DE", [P, DEC, PAGES, 2, DQ])
            DSUF = place(s, "DSUF", [P, DEC, PAGES, 2 * DQ])
            QD = place(s, "QD", [P, DEC, 2, DQ])
            NZ = place(s, "NZ", [NS, DEC, 2, DQ])
            NE = place(s, "NE", [NS, DEC, 2, DQ])
            pbias = place(s, "pbias", [P, 2])
            cap = place(s, "cap", [P, P])
            capnew = place(s, "capnew", [NS, DEC, 2, DQ])
            pt = place(s, "pt", [1, DEC * PAGES], I32)
        with ExitStack() as s:
            HH = place(s, "HH", [P, KD, T], F32R)
            HL = place(s, "HL", [P, KD, T], F32R)
            SG = [place(s, f"SG{i}", [P, CW]) for i in range(3)]
            HF = [place(s, f"HF{i}", [P, CW]) for i in range(3)]
            LSUM = place(s, "LSUM", [P, T])
        with ExitStack() as s:
            SQ = [place(s, f"SQ{i}", [P, KD, CW]) for i in range(2)]
            LS = place(s, "LS", [P, T])
            RS = place(s, "RS", [P, T])
            YT = [place(s, f"YT{i}", [P, D]) for i in range(2)]

        banks = [ctx.enter_context(nc.psum_tensor(f"bank{i}", [P, 512], F32)) for i in range(8)]

        w_raw = [sem(f"w_raw{s}") for s in range(2)]
        w_split = sem("w_split")
        d_mm = sem("d_mm")
        d_ev = sem("d_ev")
        par_load = sem("par_load")
        x_load = sem("x_load")
        set_pool = sem("set_pool")
        set_dve = sem("set_dve")
        xt_mm = sem("xt_mm")
        xt_hi = sem("xt_hi")
        xt_lo = sem("xt_lo")
        par_mm = sem("par_mm")
        par_ev = sem("par_ev")
        wt_done = sem("wt_done")
        ws_load = sem("ws_load")
        lb_max = sem("lb_max")
        lb_exp = sem("lb_exp")
        lb_own = sem("lb_own")
        s0_load = sem("s0_load")
        q_act = sem("q_act")
        sig_ready = sem("sig_ready")
        f_ready = sem("f_ready")
        k_ready = sem("k_ready")
        g_ready = sem("g_ready")
        diff_ready = sem("diff_ready")
        exp_ready = sem("exp_ready")
        x_ready = sem("x_ready")
        lev_mm = sem("lev_mm")
        lev_read = sem("lev_read")
        sc_zero = sem("sc_zero")
        vi_tr = sem("vi_tr")
        vb_ready = sem("vb_ready")
        vx_ready = sem("vx_ready")
        kt_tr = sem("kt_tr")
        kt_ready = sem("kt_ready")
        kv_mm = sem("kv_mm")
        st_chain = sem("st_chain")
        skv_mm = sem("skv_mm")
        sst_own = sem("sst_own")
        o_mm = sem("o_mm")
        o_ev = sem("o_ev")
        osq = sem("osq")
        ms_mm = sem("ms_mm")
        rms_std = sem("rms_std")
        o_own = sem("o_own")
        b_done = sem("b_done")
        u_act = sem("u_act")
        v_act = sem("v_act")
        sg_act = sem("sg_act")
        v_tr = sem("v_tr")
        v_stat = sem("v_stat")
        v_std = sem("v_std")
        v_own = sem("v_own")
        vt_ready = sem("vt_ready")
        sv_mm = sem("sv_mm")
        a_done = sem("a_done")
        ab_out = sem("ab_out")
        pt_load = sem("pt_load")
        at_pool = sem("at_pool")
        w_part = sem("w_part")
        q_hi = sem("q_hi")
        k_hi = sem("k_hi")
        qk_free = sem("qk_free")
        v_free = sem("v_free")
        pg_load = [sem(f"pg_load{i}") for i in range(4)]
        kp_tr = sem("kp_tr")
        kp_ev = sem("kp_ev")
        kp_z = sem("kp_z")
        ktok_tr = sem("ktok_tr")
        ktok_ev = sem("ktok_ev")
        vtok_tr = sem("vtok_tr")
        vtok_ev = sem("vtok_ev")
        kv_store = sem("kv_store")
        pb_ready = sem("pb_ready")
        zn_mm = sem("zn_mm")
        nz_ready = sem("nz_ready")
        nz_own = sem("nz_own")
        ne_min = sem("ne_min")
        ne_act = sem("ne_act")
        nsp_ready = sem("nsp_ready")
        rn_mm = sem("rn_mm")
        narg = sem("narg")
        nw_ready = sem("nw_ready")
        dz_ready = sem("dz_ready")
        de_min = sem("de_min")
        de_act = sem("de_act")
        dsp_ready = sem("dsp_ready")
        dsuf = sem("dsuf")
        rd_mm = sem("rd_mm")
        darg = sem("darg")
        dw_ready = sem("dw_ready")
        dv_mm = sem("dv_mm")
        do_ev = sem("do_ev")
        z_mm = sem("z_mm")
        zc = sem("zc")
        capped = sem("capped")
        e_min = sem("e_min")
        e_exp = sem("e_exp")
        e_ln = sem("e_ln")
        sp_ready = sem("sp_ready")
        sph_ready = sem("sph_ready")
        spl_ready = sem("spl_ready")
        tri_mm = sem("tri_mm")
        arg_ready = sem("arg_ready")
        carry_mm = sem("carry_mm")
        w_ready = sem("w_ready")
        pv_mm = sem("pv_mm")
        po_ev = sem("po_ev")

        m_hi = sem("m_hi")
        m_lo = sem("m_lo")
        res1 = sem("res1")
        res = sem("res")
        gate_read = sem("gate_read")
        up_read = sem("up_read")
        h_hi = sem("h_hi")
        h_lo = sem("h_lo")
        ln_zero = sem("ln_zero")
        ln_acc = sem("ln_acc")
        ln_mean = sem("ln_mean")
        ln_cent = sem("ln_cent")
        ln_sq = sem("ln_sq")
        ln_sum2 = sem("ln_sum2")
        ln_var = sem("ln_var")
        ln_std = sem("ln_std")
        ln_rstd = sem("ln_rstd")
        ln_norm = sem("ln_norm")
        ln_aff = sem("ln_aff")
        x_hi = sem("x_hi")
        x_lo = sem("x_lo")
        y_tr = sem("y_tr")
        y_ev = sem("y_ev")
        y_out = [sem(f"y_out{i}") for i in range(2)]

        out_stages = []
        for l in range(2):
            out_stages.append((("about", "cout")[l], KD, HH, None, l))
            out_stages += [(("down", l, g), k, HH, g, l) for g, (_, k) in enumerate(GROUPS)]
        units, scaled, n1, n2 = {}, {}, 0, 0
        for name, _, _, g, _ in out_stages:
            units[name], scaled[name] = n1, n2
            n1 += 3 * KD
            n2 += 3 * KD if not g else 0
        ln_units = {}
        for n, name in enumerate(["about", ("down", 0, 2), "cout", ("down", 1, 2)]):
            ln_units[n] = (units[name] + 3 * KD, scaled[name] + (3 * KD if n % 2 == 0 else 0))
        ffn_pairs = {}
        n1 = 0
        for l in range(2):
            for g, (_, k) in enumerate(GROUPS):
                ffn_pairs[l, g] = n1
                n1 += k

        STEPS = [(h, c, b) for h in range(2) for c in (1, 0) for b in range(4 * c + 3, -1, -1)]
        NST = len(STEPS)
        LOW = [max(b * P - 512 * c, 0) for _, c, b in STEPS]
        DIAG = [b >= 4 * c for _, c, b in STEPS]
        FIRST = [b == 4 * c + 3 for _, c, b in STEPS]
        FINAL = [b == 0 for _, c, b in STEPS]
        carries = lambda s: sum(not f for f in FINAL[:s + 1])
        NCARRY = carries(NST - 1)
        chunks_done = lambda s: sum(FINAL[:s + 1])
        ck_v = cache_k[0].rearrange("g p h d -> g p (h d)")
        cv_v = cache_v[0].rearrange("g p h d -> g p (h d)")
        N_POOL = cache_k.shape[1]
        ckp_v, cvp_v = (a[0, 0].rearrange("(n p) h d -> p n (h d)", p=P) for a in (ck_prompt, cv_prompt))
        cks_v, cvs_v = (a[0].rearrange("n t h d -> (n t) (h d)") for a in (ck_sample, cv_sample))

        Q_FIRST, Q_COUNT = 8, 9
        GROUPS_AT = ((0, 1), (2, 3), (4, 5), (6, 7), (8, 9), (10,))
        LATE_GROUPS = (11, 12, 13, 14, 15)
        LAST_LN = 2 * LAYERS - 1
        VBANK = (6, 7)
        VARB = (6, 7, 3)
        AB_COLS = (8, 12, 16, 20, 0, 4)
        PROWS, LROWS, BROW = EX[0][0:64, 0:P], EX[1][0:13, 0:P], Q[0:1, 0:1040]
        s0_v = state_b[0].rearrange("n h k v -> k h n v")
        s0o_v = state_b_sample[0].rearrange("n h k v -> k h n v")
        av_v = a_v_sample[0].rearrange("n t (h d) -> (n t) h d", h=HB)
        sbp_v = state_b_prompt[0, 0].rearrange("h k v -> k h v")

        block = ctx.enter_context(nc.Block())
        flat = lambda a: a.rearrange("p k t -> p (k t)")
        wv = lambda w, l: w[l].rearrange("(k p) (n c) -> p n k c", p=P, c=P)
        w_ab, w_abo = wv(ab_w_in, 0), wv(ab_w_out, 0)
        w_c, w_co = wv(c_w_in, 0), wv(c_w_out, 0)
        w_gate, w_up, w_down = ([wv(w, l) for l in range(2)] for w in (ffn_w_gate, ffn_w_up, ffn_w_down))
        XP = flat(R)[:, 0:NP * D].rearrange("p (n d) -> p n d", n=NP)

        @block.sync
        def _(sp):
            for k in range(NP):
                sp.dma_start(XP[:, k, :], x_prompt[0, k * P:(k + 1) * P, :]).then_inc(x_load, 16)
            sp.dma_start(XS, x_sample.rearrange("n t d -> (n t) d")).then_inc(x_load, 16)
            for i, w in enumerate((ln1_g, ln1_b, ln2_g, ln2_b)):
                sp.dma_start(PROWS[16 * i:16 * i + 16, :], w.rearrange("l (k p) -> (l k) p", p=P)).then_inc(par_load, 16)
            sp.dma_start(LROWS[0:12, :], b_lb_logits.rearrange("r (h p) -> (r h) p", p=P)).then_inc(par_load, 16)
            sp.dma_start(LROWS[12:13, :], b_norm_g).then_inc(par_load, 16)
            sp.dma_start(BROW[:, 0:512], a_ln_g).then_inc(par_load, 16)
            sp.dma_start(BROW[:, 512:1024], a_ln_b).then_inc(par_load, 16)
            sp.dma_start(BROW[:, 1024:1040], c_logit_bias).then_inc(par_load, 16)
            sp.dma_start(KT[:, 0:HB, :], a_w_s[0].rearrange("h t s -> t h s")).then_inc(par_load, 16)
            sp.dma_start(bsrow[:], a_b_s).then_inc(par_load, 16)
            sp.wait_ge(wt_done, 1)
            for n in range(DEC):
                sp.dma_start(WS[DQ * n:DQ * n + DQ, :, DQ * n:DQ * n + DQ], WT[0:DQ, :, 0:DQ]).then_inc(ws_load, 16)

            def stream(stage, pairs, kb, k0, cols, first=0):
                with sp.Fori(first, pairs) as j:
                    for s in range(2):
                        w, col = cols(j, s)
                        col = sp.snap(col)
                        sp.wait_ge(w_split, 2 * TB[stage] + 4 * j + 2 * s + 1)
                        sp.dma_start(RAW[s][:, 0:kb, :], w[:, bass.ds(col, 1), k0:k0 + kb]
                                     .rearrange("p n k c -> p (n k) c")).then_inc(w_raw[s], 16)

            def attention_loads():
                base = TB["c"]

                def tile(hp, j, nxt):
                    col = sp.snap(hp + nxt + NPAIR * j)
                    sp.wait_ge(w_split, 2 * base + 6 * (hp + nxt) + 2 * j + (2 if j == 0 else 0) + 1)
                    sp.dma_start(RAW[j % 2][:], w_c[:, bass.ds(col, 1)].rearrange("p n k c -> p (n k) c"))\
                      .then_inc(w_raw[j % 2], 16)

                def pages(hp, view, m):
                    _, ids = nc.values_load_multi_w_load_instructions(
                        pt[0:1, PAGES * m:PAGES * (m + 1)], engines=[mybir.EngineType.SP], min_val=0, max_val=N_POOL - 1)
                    first = sp.snap(hp * P)
                    if (view is ck_v) == (m < 4):
                        sp.wait_ge(dv_mm, DEC * hp + m + 1)
                    else:
                        sp.wait_ge(kp_tr, 16 * hp + 2 * ((m + 4) % DEC) + 3)
                    for g in range(PAGES):
                        sp.dma_start(PG[m % 4][:, g, :], view[bass.ds(ids[g], 1), :, bass.ds(first, P)]
                                     .rearrange("o p c -> (o p) c")).then_inc(pg_load[m % 4], 16)

                def pair(hp, last):
                    tile(hp, 2, 0)
                    for m in range(4, DEC):
                        pages(hp, ck_v, m)
                    if last:
                        for j in range(2):
                            sp.wait_ge(w_split, 2 * TB["cout"] + 2 * j + (2 if j == 0 else 0) + 1)
                            sp.dma_start(RAW[j][:], w_co[:, j]).then_inc(w_raw[j], 16)
                    else:
                        for j in range(2):
                            tile(hp, j, 1)
                    for m in range(4):
                        pages(hp, cv_v, m)
                    for a, b, tok, ev in ((ckp_v, cks_v, KTOK, ktok_ev), (cvp_v, cvs_v, VTOK, vtok_ev)):
                        sp.wait_ge(ev, 3 * hp + 3)
                        sp.dma_start(a[:, :, bass.ds(2 * hp * (P // 2), P)], tok[:, 0:NP, :]).then_inc(kv_store, 16)
                        sp.dma_start(b[:, bass.ds(2 * hp * (P // 2), P)], tok[0:NS, NP, :]).then_inc(kv_store, 16)
                    for m in range(4, DEC):
                        pages(hp, cv_v, m)
                    if not last:
                        for m in range(4):
                            pages(hp + 1, ck_v, m)

                for j in range(2):
                    tile(0, j, 0)
                sp.wait_ge(at_pool, 3)
                sp.dma_start(pt[:], page_table.rearrange("(o n) g -> o (n g)", o=1)).then_inc(pt_load, 16)
                sp.wait_ge(pt_load, 16)
                for m in range(4):
                    pages(0, ck_v, m)
                with sp.Fori(0, NPAIR - 1) as hp:
                    pair(hp, False)
                pair(NPAIR - 1, True)

            with sp.Fori(0, HB) as h:
                for j, first in enumerate(AB_COLS):
                    col = sp.snap(h + first)
                    sp.wait_ge(w_split, 12 * h + 2 * j + 1)
                    sp.dma_start(RAW[j % 2][:], w_ab[:, bass.ds(col, 1)].rearrange("p n k c -> p (n k) c"))\
                      .then_inc(w_raw[j % 2], 16)
            for l in range(LAYERS):
                if l == 0:
                    stream("about", KD // 2, KD, 0, lambda j, s: (w_abo, 2 * j + s))
                else:
                    attention_loads()
                    stream("cout", KD // 2, KD, 0, lambda j, s: (w_co, 2 * j + s), 1)
                for g, (b0, k) in enumerate(GROUPS):
                    stream(("up", l, g), k, KD, 0, lambda j, s: ((w_gate[l], w_up[l])[s], j + b0))
                    stream(("down", l, g), KD // 2, k, b0, lambda j, s: (w_down[l], 2 * j + s))

            for n in range(NP + 1):
                sp.wait_ge(y_ev, 2 * n + 2)
                rows = P if n < NP else NS
                to = y_prompt[0, n * P:(n + 1) * P, :] if n < NP else y_sample.rearrange("n t d -> (n t) d")
                sp.dma_start(to, YT[n % 2][0:rows, :]).then_inc(y_out[n % 2], 16)
            sp.wait_ge(y_out[0], 16 * (NP // 2 + 1))
            sp.wait_ge(y_out[1], 16 * (NP // 2))
            sp.wait_ge(ab_out, 48 * HB + 16)

        @block.gpsimd
        def _(pool):
            nc.gpsimd.memset(zero[:], 0.0).then_inc(set_pool, 1)
            nc.gpsimd.memset(ident[:], 0.0).then_inc(set_pool, 1)
            nc.gpsimd.memset(tri[:], 1.0).then_inc(set_pool, 1)
            nc.gpsimd.memset(levmask[:], 0.0).then_inc(set_pool, 1)
            nc.gpsimd.memset(sel[:], 1.0).then_inc(set_pool, 1)
            nc.gpsimd.memset(WS[:], 0.0).then_inc(set_pool, 1)
            pool.wait_ge(set_pool, 6)
            nc.gpsimd.affine_select(out=ident[:], in_=ident[:], compare_op=ALU.not_equal, fill=1.0, base=0,
                                    pattern=[[-1, P]], channel_multiplier=1).then_inc(set_pool, 1)
            nc.gpsimd.affine_select(out=tri[:], in_=tri[:], compare_op=ALU.is_ge, fill=0.0, base=0,
                                    pattern=[[-1, P]], channel_multiplier=1).then_inc(set_pool, 1)
            nc.gpsimd.affine_select(out=sel[:], in_=sel[:], compare_op=ALU.is_ge, fill=0.0, base=0,
                                    pattern=[[-DQ, DEC]], channel_multiplier=1).then_inc(set_pool, 1)
            pool.wait_ge(set_pool, 9)
            nc.gpsimd.affine_select(out=sel[:], in_=sel[:], compare_op=ALU.is_ge, fill=0.0, base=DQ - 1,
                                    pattern=[[DQ, DEC]], channel_multiplier=-1).then_inc(set_pool, 1)
            for i, w in enumerate(LEVELS):
                late = levmask[:, i, :].rearrange("p (n a r) -> p n a r", a=2, r=w)[:, :, 1, :]
                nc.gpsimd.memset(late, 1.0).then_inc(set_pool, 1)
            pool.wait_ge(set_pool, 17)
            for i, w in enumerate(LEVELS):
                late = levmask[:, i, :].rearrange("p (n a r) -> p n a r", a=2, r=w)[:, :, 1, :]
                nb = P // (2 * w)
                nc.gpsimd.affine_select(out=late, in_=late, compare_op=ALU.is_ge, fill=0.0, base=0,
                                        pattern=[[-2 * w, nb], [0, w]], channel_multiplier=1).then_inc(set_pool, 1)
                pool.wait_ge(set_pool, 18 + 2 * i)
                nc.gpsimd.affine_select(out=late, in_=late, compare_op=ALU.is_ge, fill=0.0, base=w - 1,
                                        pattern=[[2 * w, nb], [0, w]], channel_multiplier=-1).then_inc(set_pool, 1)
            pool.wait_ge(par_ev, 5)
            nc.gpsimd.affine_select(out=WT[:], in_=WT[:], compare_op=ALU.is_ge, fill=0.0, base=0,
                                    pattern=[[0, HB], [1, P]], channel_multiplier=-1).then_inc(wt_done, 1)

            def split(slot, kb, loads, before, used):
                pool.wait_ge(w_raw[slot], 16 * loads)
                pool.wait_ge(d_mm, 3 * used + 1)
                nc.gpsimd.tensor_tensor(WH[slot][:, 0:kb, :], RAW[slot][:, 0:kb, :],
                                        zero[:].to_broadcast([P, kb, P]), ALU.add).then_inc(w_split, 1)
                pool.wait_ge(w_split, before + 4)
                nc.gpsimd.tensor_tensor(WL[slot][:, 0:kb, :], RAW[slot][:, 0:kb, :],
                                        WH[slot][:, 0:kb, :].bitcast(F32), ALU.subtract).then_inc(w_split, 1)

            def split_pair(stage, kb, j):
                n = TB[stage]
                l0, l1 = SLOT_LOADS[stage]
                split(0, kb, l0 + j + 1, 2 * n + 4 * j, n + 2 * j)
                split(1, kb, l1 + j + 1, 2 * n + 4 * j + 2, n + 2 * j + 1)

            def splits(stage, pairs, kb, first=0):
                with pool.Fori(first, pairs) as j:
                    split_pair(stage, kb, j)

            with pool.Fori(0, HB) as h:
                for j in range(6):
                    split(j % 2, KD, 3 * h + j // 2 + 1, 12 * h + 2 * j, 6 * h + j)

            def attention_pool():
                pool.wait_ge(ln_norm, 6)
                nc.gpsimd.memset(cap[:], 1e30).then_inc(at_pool, 1)
                nc.gpsimd.memset(capnew[:], 1e30).then_inc(at_pool, 1)
                nc.gpsimd.memset(QD[:], 0.0).then_inc(at_pool, 1)
                pool.wait_ge(at_pool, 3)
                nc.gpsimd.affine_select(out=cap[:], in_=cap[:], compare_op=ALU.is_ge, fill=MASKED, base=-1,
                                        pattern=[[1, P]], channel_multiplier=-1).then_inc(at_pool, 1)
                for h in range(2):
                    nc.gpsimd.affine_select(out=capnew[:, :, h, :], in_=capnew[:, :, h, :], compare_op=ALU.is_ge, fill=MASKED,
                                            base=0, pattern=[[-DQ, DEC], [0, DQ]], channel_multiplier=1).then_inc(at_pool, 1)
                pool.wait_ge(at_pool, 6)
                for h in range(2):
                    nc.gpsimd.affine_select(out=capnew[:, :, h, :], in_=capnew[:, :, h, :], compare_op=ALU.is_ge, fill=MASKED,
                                            base=-1, pattern=[[DQ, DEC], [1, DQ]], channel_multiplier=-1).then_inc(at_pool, 1)
                def split_part(slot, k, loads, parts, used):
                    if k == 0:
                        pool.wait_ge(w_raw[slot], 16 * loads)
                        pool.wait_ge(d_mm, 3 * used + 1)
                    nc.gpsimd.tensor_tensor(WH[slot][:, k, :], RAW[slot][:, k, :], zero[:].to_broadcast([P, P]),
                                            ALU.add).then_inc(w_part, 1)
                    pool.wait_ge(w_part, parts + 1)
                    rest = nc.gpsimd.tensor_tensor(WL[slot][:, k, :], RAW[slot][:, k, :], WH[slot][:, k, :].bitcast(F32),
                                                   ALU.subtract)
                    if k == KD - 1:
                        rest.then_inc(w_split, 2)

                n0 = TB["c"]
                l0, l1 = SLOT_LOADS["c"]
                with pool.Fori(0, NPAIR) as hp:
                    n = n0 + 3 * hp
                    split(0, KD, l0 + 2 * hp + 2, 2 * n + 4, n + 2)
                    for s in range(NST):
                        c = slice(LOW[s], 512)
                        pool.wait_ge(sph_ready, NST * hp + s + 1)
                        if s >= 2:
                            if FINAL[s - 2]:
                                pool.wait_ge(tri_mm, NST * hp + s - 1)
                            else:
                                pool.wait_ge(carry_mm, NCARRY * hp + carries(s - 2))
                        nc.gpsimd.tensor_tensor(SPL[s % 2][:, c], E[s % 2][:, c], SPH[s % 2][:, c].bitcast(F32),
                                                ALU.subtract).then_inc(spl_ready, 1)
                        if 1 <= s < 5:
                            for k in (2 * s - 2, 2 * s - 1):
                                split_part(0, k, l0 + 2 * hp + 3, 16 * hp + k, n + 4)
                        elif 8 <= s < 8 + KD:
                            split_part(1, s - 8, l1 + hp + 2, 16 * hp + s, n + 3)

            def norm_rest(n):
                pool.wait_ge(x_hi, 3 * n + 1)
                nc.gpsimd.tensor_tensor(XL[:, :, CH[0]], R[:, :, CH[0]], XH[:, :, CH[0]].bitcast(F32),
                                        ALU.subtract).then_inc(x_lo, 1)

            for l in range(LAYERS):
                if l == 0:
                    splits("about", KD // 2, KD)
                else:
                    attention_pool()
                    splits("cout", KD // 2, KD, 1)
                split_pair(("up", l, 0), KD, 0)
                norm_rest(2 * l)
                for g, (_, k) in enumerate(GROUPS):
                    splits(("up", l, g), k, KD, 0 if g else 1)
                    splits(("down", l, g), KD // 2, k)
                if 2 * l + 1 < LAST_LN:
                    l0, l1 = SLOT_LOADS["c"]
                    split(0, KD, l0 + 1, 2 * TB["c"], TB["c"])
                    split(1, KD, l1 + 1, 2 * TB["c"] + 2, TB["c"] + 1)
                    norm_rest(2 * l + 1)

        @block.scalar
        def _(act):
            for k in range(KD):
                act.wait_ge(xt_mm, k + 1)
                for i, c in enumerate((slice(0, 512), slice(512, SEQ), slice(SEQ, T))):
                    n = c.stop - c.start
                    last = nc.scalar.activation(XH[:, k, c], banks[3 * (k % 2) + i][:, 0:n], ACT.Copy)
                last.then_inc(xt_hi, 1)
            act.wait_ge(lb_max, 4)
            nc.scalar.activation(lbw[:, 4:16], lbw[:, 4:16], ACT.Exp).then_inc(lb_exp, 1)

            def copy_out(c, n, to):
                act.wait_ge(d_mm, n + c + 5)
                nc.scalar.activation(to[:, CH[c]], banks[c][:, 0:CW], ACT.Copy).then_inc(d_ev, 1)

            def level_exp(h, i):
                w = LEVELS[i] if i < 7 else P
                act.wait_ge(diff_ready, 8 * h + i + 1)
                e = EX[i % 2][:, 0:SEQ if 2 < w < P else T]
                nc.scalar.activation(e, e, ACT.Exp).then_inc(exp_ready, 1)

            with act.Fori(0, HB) as h:
                n = 18 * h
                for c in range(3):
                    copy_out(c, n, Q)
                act.wait_ge(d_ev, n + 6)
                nc.scalar.activation(Q[:], Q[:], ACT.Silu).then_inc(q_act, 1)
                for c in range(3):
                    copy_out(c, n + 3, EX[1])
                act.wait_ge(d_ev, n + 9)
                act.wait_ge(b_done, h + 1)
                nc.scalar.activation(K[:], EX[1][:], ACT.Sigmoid, scale=-1.0).then_inc(sig_ready, 1)
                nc.scalar.activation(G[:], EX[1][:], ACT.Sigmoid).then_inc(sig_ready, 1)
                act.wait_ge(sig_ready, 2 * h + 2)
                nc.scalar.activation(EX[1][:], G[:], ACT.Ln, scale=lbw[:, bass.ds(h + 28, 1)],
                                     bias=lbw[:, bass.ds(h + 24, 1)]).then_inc(f_ready, 1)
                for c in range(3):
                    copy_out(c, n + 6, U)
                act.wait_ge(ab_out, 48 * h + 16)
                act.dma_start(S0[:], s0_v[:, bass.ds(h, 1)].rearrange("k h n v -> k (h n) v")).then_inc(s0_load, 16)
                act.wait_ge(vi_tr, 3 * h + 4)
                level_exp(h, 0)
                for i in range(9):
                    if i < 6:
                        level_exp(h, i + 1)
                    copy_out(i % 3, n + 9 + i - i % 3, (SGG, U, V)[i // 3])
                act.wait_ge(lev_mm, 8 * h + 6)
                nc.scalar.activation(EX[1][:], G[:], ACT.Exp).then_inc(exp_ready, 1)
                act.wait_ge(diff_ready, 8 * h + 8)
                nc.scalar.activation(EX[0][:], EX[0][:], ACT.Exp).then_inc(exp_ready, 1)
                nc.scalar.activation(DG[:, 0, :], G[:, P - 1:SEQ:P], ACT.Exp).then_inc(exp_ready, 1)
                nc.scalar.activation(DG[:, 1, :], G[:, SEQ + DQ - 1:T:DQ], ACT.Exp).then_inc(exp_ready, 1)
                act.wait_ge(d_ev, n + 21)
                nc.scalar.activation(V[:], V[:], ACT.Gelu_apprx_tanh).then_inc(v_act, 1)
                nc.scalar.activation(U[:], U[:], ACT.Gelu_apprx_tanh).then_inc(u_act, 1)
                nc.scalar.activation(SGG[:], SGG[:], ACT.Silu).then_inc(sg_act, 1)
                act.wait_ge(v_stat, h + 1)
                nc.scalar.activation(brs[:], bmv[:, :, 1], ACT.Sqrt, bias=epsln[:]).then_inc(v_std, 1)
                act.wait_ge(vt_ready, 2 * h + 2)
                act.dma_start(av_v[:, bass.ds(h, 1)].rearrange("t h d -> t (h d)"), VT[0:NS, NP, :]).then_inc(ab_out, 16)
                act.wait_ge(st_chain, 8 * h + 8)
                act.dma_start(sbp_v[:, bass.ds(h, 1)].rearrange("k h v -> k (h v)"), SS[:, NP - 1, :]).then_inc(ab_out, 16)
                act.wait_ge(o_mm, h + 2)
                for i, (b, c) in enumerate(((6, slice(0, 512)), (7, slice(512, SEQ)), (5, slice(SEQ, T)))):
                    nc.scalar.activation(K[:, c], banks[b][:, 0:c.stop - c.start], ACT.Copy).then_inc(o_ev, 1)
                act.wait_ge(o_ev, 3 * h + 3)
                nc.scalar.activation(G[:], K[:], ACT.Square).then_inc(osq, 1)
                act.wait_ge(ms_mm, h + 1)
                for c in range(3):
                    nc.scalar.activation(EX[0][:, CH[c]], banks[3 + c][:, 0:CW], ACT.Sqrt, bias=epsrms[:],
                                         scale=1.0 / P).then_inc(rms_std, 1)
                act.wait_ge(sst_own, 3 * h + 3)
                act.dma_start(s0o_v[:, bass.ds(h, 1)].rearrange("k h n v -> k (h n) v"), S0[:]).then_inc(ab_out, 16)

            act.wait_ge(b_done, HB + 1)
            act.wait_ge(a_done, HB)
            act.wait_ge(ab_out, 48 * HB + 16)
            for c in range(3):
                nc.scalar.activation(HH[:, :, CH[c]], R[:, :, CH[c]], ACT.Copy).then_inc(m_hi, 1)

            def attention_act():
                act.wait_ge(at_pool, 8)
                nc.scalar.preload_act_table_set("natural_log_exp_and_others")
                with act.Fori(0, NPAIR) as hp:
                    n = 3 * (TB["c"] + 3 * hp)
                    nc.scalar.activation(pbias[:], cbias[:, bass.ds(2 * hp, 2)], ACT.Copy).then_inc(pb_ready, 1)
                    for c in range(3):
                        act.wait_ge(d_mm, n + c + 5)
                        if c == 2:
                            for h in range(2):
                                r = slice(64 * h, 64 * h + 64)
                                nc.scalar.activation(QD[r, :, h, :], banks[2][r, CW - NS:CW].rearrange("p (n i) -> p n i", i=DQ),
                                                     ACT.Copy, scale=0.125)
                        nc.scalar.activation(QH[:, CH[c]], banks[c][:, 0:CW], ACT.Copy, scale=0.125).then_inc(q_hi, 1)
                    for c in range(3):
                        act.wait_ge(d_mm, n + 3 + c + 5)
                        nc.scalar.activation(KF[:, CH[c]], banks[c][:, 0:CW], ACT.Copy)
                        nc.scalar.activation(KH[:, CH[c]], banks[c][:, 0:CW], ACT.Copy).then_inc(k_hi, 1)
                    for c in range(3):
                        act.wait_ge(d_mm, n + 6 + c + 5)
                        nc.scalar.activation(VI[:, CH[c]], banks[c][:, 0:CW], ACT.Copy).then_inc(v_free, 1)
                    def logits(s):
                        if s >= 4:
                            act.wait_ge(pv_mm, NST * hp + s - 3)
                        act.wait_ge(z_mm, NST * hp + s + 1)
                        c, h = slice(LOW[s], 512), STEPS[s][0]
                        nc.scalar.activation(Z[s % 4][:, c], banks[6 + s % 2][:, c], ACT.Identity,
                                             bias=pbias[:, h:h + 1]).then_inc(zc, 1)

                    def log1p_exp(s):
                        e = E[s % 2][:, LOW[s]:512]
                        act.wait_ge(e_min, NST * hp + s + 1)
                        nc.scalar.activation(e, e, ACT.Exp).then_inc(e_exp, 1)
                        act.wait_ge(e_exp, NST * hp + s + 1)
                        nc.scalar.activation(e, e, ACT.Ln, bias=1.0).then_inc(e_ln, 1)

                    def weights(s):
                        z = Z[s % 4][:, LOW[s]:512]
                        act.wait_ge(arg_ready, NST * hp + s + 1)
                        nc.scalar.activation(z, z, ACT.Exp).then_inc(w_ready, 1)

                    def output(s):
                        h, c, _ = STEPS[s]
                        r = slice(64 * h, 64 * h + 64)
                        act.wait_ge(pv_mm, NST * hp + s + 1)
                        nc.scalar.activation(R[r, bass.ds(hp, 1), 512 * c:512 * c + 512].rearrange("p k t -> p (k t)"),
                                             banks[4][r, :], ACT.Copy).then_inc(po_ev, 1)

                    logits(0)
                    for s in range(-2, NST + 1):
                        if 0 <= s + 2 < NST:
                            log1p_exp(s + 2)
                        if 0 <= s < NST:
                            weights(s)
                        if s >= 1 and FINAL[s - 1]:
                            output(s - 1)
                        if s + 3 < NST:
                            logits(s + 3)
                        if s == -2:
                            act.wait_ge(kv_store, 64 * hp + 16)
                            for b in range(2):
                                act.wait_ge(vtok_tr, 3 * hp + b + 1)
                                nc.scalar.activation(VTOK[:, 4 * b:4 * b + 4, :].rearrange("p n c -> p (n c)"), banks[b][:],
                                                     ACT.Copy).then_inc(vtok_ev, 1)
                            act.wait_ge(vtok_tr, 3 * hp + 3)
                            nc.scalar.activation(VTOK[0:NS, NP, :], banks[2][0:NS, 0:P], ACT.Copy).then_inc(vtok_ev, 1)
                            act.wait_ge(pb_ready, hp + 1)
                            act.wait_ge(zn_mm, hp + 1)
                            for h in range(2):
                                nc.scalar.activation(NZ[:, :, h, :], banks[4][0:NS, 0:64].rearrange("p (n h i) -> p n h i", h=2, i=DQ)[:, :, h, :],
                                                     ACT.Identity, bias=pbias[0:NS, h:h + 1]).then_inc(nz_ready, 1)
                            act.wait_ge(kp_z, 16 * hp + 16)
                            for h in range(2):
                                nc.scalar.activation(DZ[:, :, :, h, :].rearrange("p n g i -> p (n g) i"),
                                                     banks[5][:].rearrange("p (m h i) -> p m h i", h=2, i=DQ)[:, :, h, :],
                                                     ACT.Identity, bias=pbias[:, h:h + 1]).then_inc(dz_ready, 1)
                        if s == -1:
                            for e, m, a in ((NE, ne_min, ne_act), (DE, de_min, de_act)):
                                act.wait_ge(m, hp + 1)
                                nc.scalar.activation(e[:], e[:], ACT.Exp).then_inc(a, 1)
                                act.wait_ge(a, 2 * hp + 1)
                                nc.scalar.activation(e[:], e[:], ACT.Ln, bias=1.0).then_inc(a, 1)
                        if s == 8:
                            act.wait_ge(narg, hp + 2)
                            nc.scalar.activation(NE[:], NZ[:], ACT.Exp).then_inc(nw_ready, 1)
                            act.wait_ge(darg, hp + 1)
                            nc.scalar.activation(DE[:], DZ[:], ACT.Exp).then_inc(dw_ready, 1)
                    act.wait_ge(dv_mm, DEC * hp + DEC + 4)
                    for h in range(2):
                        r = slice(64 * h, 64 * h + 64)
                        nc.scalar.activation(R[r, bass.ds(hp, 1), SEQ:T].rearrange("p k (n i) -> p (k n) i", i=DQ),
                                             banks[5][r, 0:64].rearrange("p (n h i) -> p n h i", h=2, i=DQ)[:, :, h, :],
                                             ACT.Copy).then_inc(do_ev, 1)
                act.wait_ge(kv_store, 64 * NPAIR + 16)
                act.wait_ge(po_ev, 4 * NPAIR + 1)
                act.wait_ge(do_ev, 2 * NPAIR + 1)
                for c in range(3):
                    nc.scalar.activation(HH[:, :, CH[c]], R[:, :, CH[c]], ACT.Copy).then_inc(m_hi, 1)

            def norm_act(n):
                l, o = n // 2, 2 * (n % 2)
                def square(c):
                    act.wait_ge(ln_cent, 3 * n + c + 1)
                    if c == 2:
                        act.wait_ge(ln_sum2, 3 * n + 1)
                    nc.scalar.activation(SQ[c % 2][:], R[:, :, CH[c]], ACT.Square).then_inc(ln_sq, 1)

                def deviation(c):
                    act.wait_ge(ln_var, 3 * n + c + 1)
                    nc.scalar.activation(RS[:, CH[c]], banks[VARB[c]][:, 0:CW], ACT.Sqrt, bias=epsln[:], scale=1.0 / D).then_inc(ln_std, 1)

                def affine(c):
                    act.wait_ge(ln_norm, 3 * n + c + 1)
                    for k in range(KD):
                        nc.scalar.activation(R[:, k, CH[c]], R[:, k, CH[c]], ACT.Identity,
                                             scale=lnp[:, o, l, k:k + 1], bias=lnp[:, o + 1, l, k:k + 1])\
                          .then_inc(ln_aff, 1)
                    if n < LAST_LN:
                        act.wait_ge(ln_aff, 24 * n + 8 * c + 8)
                        nc.scalar.activation(XH[:, :, CH[c]], R[:, :, CH[c]], ACT.Copy).then_inc(x_hi, 1)

                square(0)
                square(1)
                deviation(0)
                square(2)
                deviation(1)
                affine(0)
                deviation(2)
                affine(1)
                affine(2)

            for l in range(LAYERS):
                if l == 1:
                    attention_act()
                norm_act(2 * l)
                for g, (_, kg) in enumerate(GROUPS):
                    done = ffn_pairs[l, g]
                    if g:
                        act.wait_ge(d_mm, 3 * (TB["down", l, g - 1] + KD) + 4)
                    with act.Fori(0, kg) as j:
                        for c in range(3):
                            act.wait_ge(d_mm, 3 * TB["up", l, g] + 6 * j + c + 5)
                            act.wait_ge(up_read, 3 * done + 3 * j + c + 1)
                            nc.scalar.activation(SG[c][:], banks[c][:, 0:CW], ACT.Silu).then_inc(gate_read, 1)
                        for c in range(3):
                            act.wait_ge(up_read, 3 * done + 3 * j + c + 4)
                            nc.scalar.activation(HH[:, bass.ds(j, 1), CH[c]].rearrange("p k t -> p (k t)"),
                                                 HF[c][:], ACT.Copy).then_inc(h_hi, 1)
                norm_act(2 * l + 1)

        @block.vector
        def _(dve):
            v = nc.vector
            v.memset(ones[:], 1.0).then_inc(set_dve, 1)
            v.memset(epsln[:], LN_EPS).then_inc(set_dve, 1)
            v.memset(epsrms[:], RMS_EPS).then_inc(set_dve, 1)
            v.memset(bmv[:], 1.0).then_inc(set_dve, 1)
            v.memset(resets[:], 1.0).then_inc(set_dve, 1)
            dve.wait_ge(set_dve, 5)
            v.memset(resets[:, 0:SEQ:P], 0.0).then_inc(set_dve, 1)
            v.memset(resets[:, SEQ:T:DQ], 0.0).then_inc(set_dve, 1)
            started = ((w_split, 2 + 1), (d_mm, 3 + 1), (d_ev, 3), (res1, 3), (up_read, 3), (h_lo, 3), (v_free, 3),
                       (ln_acc, 3), (lev_read, 1), (dv_mm, 4), (kp_tr, 1), (b_done, 1), (kt_tr, 1), (vi_tr, 1),
                       (o_mm, 1), (rms_std, 1), (narg, 1), (po_ev, 1), (do_ev, 1), (ab_out, 16), (kv_store, 16))
            for i, (semaphore, count) in enumerate(started):
                v.memset(credit[:, i:i + 1], 0.0).then_inc(semaphore, count)
            dve.wait_ge(set_pool, 31)
            v.tensor_copy(triR[:], tri[:]).then_inc(set_dve, 1)
            v.tensor_scalar(restR[:], tri[:], -1.0, 1.0, ALU.mult, ALU.add).then_inc(set_dve, 1)
            dve.wait_ge(par_mm, 5)
            v.tensor_copy(lnp[:].rearrange("p a l k -> p (a l k)"), banks[6][:, 0:64]).then_inc(par_ev, 1)
            v.tensor_copy(lbp[:, 0:13], banks[6][:, 64:77]).then_inc(par_ev, 1)
            v.tensor_copy(cbias[:], banks[6][:, 128:144]).then_inc(par_ev, 1)
            v.tensor_copy(WT[:].rearrange("p h s -> p (h s)"), banks[7][:]).then_inc(par_ev, 2)
            for k in range(KD):
                dve.wait_ge(xt_hi, k + 1)
                for i, c in enumerate((slice(0, 512), slice(512, SEQ), slice(SEQ, T))):
                    n = c.stop - c.start
                    last = v.tensor_tensor(XL[:, k, c], banks[3 * (k % 2) + i][:, 0:n], XH[:, k, c].bitcast(F32),
                                           ALU.subtract)
                last.then_inc(xt_lo, 1)
            dve.wait_ge(par_mm, 7)
            v.tensor_copy(gainA[:].rearrange("p h d -> p (h d)"), banks[6][:]).then_inc(par_ev, 1)
            v.tensor_copy(biasA[:].rearrange("p h d -> p (h d)"), banks[7][:]).then_inc(par_ev, 1)
            dve.wait_ge(par_load, 16 * 11)
            v.tensor_copy(bsS[:], bsrow[:, :, None, 0:DQ].to_broadcast([1, HB, DEC, DQ])).then_inc(par_ev, 1)
            dve.wait_ge(par_ev, 5)
            v.tensor_tensor(lbw[:, 0:4], lbp[:, 0:4], lbp[:, 4:8], ALU.max).then_inc(lb_max, 1)
            dve.wait_ge(lb_max, 1)
            v.tensor_tensor(lbw[:, 0:4], lbw[:, 0:4], lbp[:, 8:12], ALU.max).then_inc(lb_max, 1)
            dve.wait_ge(lb_max, 2)
            v.tensor_tensor(lbw[:, 4:16].rearrange("p (r h) -> p r h", r=3), lbp[:, 0:12].rearrange("p (r h) -> p r h", r=3),
                            lbw[:, None, 0:4].to_broadcast([P, 3, 4]), ALU.subtract).then_inc(lb_max, 2)
            dve.wait_ge(lb_exp, 1)
            v.tensor_tensor(lbw[:, 16:20], lbw[:, 4:8], lbw[:, 8:12], ALU.add).then_inc(lb_own, 1)
            dve.wait_ge(lb_own, 1)
            v.tensor_tensor(lbw[:, 16:20], lbw[:, 16:20], lbw[:, 12:16], ALU.add).then_inc(lb_own, 1)
            dve.wait_ge(lb_own, 2)
            v.reciprocal(lbw[:, 20:24], lbw[:, 16:20]).then_inc(lb_own, 1)
            dve.wait_ge(lb_own, 3)
            v.tensor_tensor(lbw[:, 24:28], lbw[:, 4:8], lbw[:, 20:24], ALU.mult).then_inc(lb_own, 1)
            dve.wait_ge(lb_own, 4)
            v.tensor_scalar(lbw[:, 28:32], lbw[:, 24:28], -1.0, 1.0, ALU.mult, ALU.add).then_inc(lb_own, 1)
            dve.wait_ge(lb_own, 5)

            def halves(a, w, n):
                return a[:, 0:n].rearrange("p (n a w) -> p n a w", a=2, w=w)

            def diff(h, i):
                w = LEVELS[i]
                n = SEQ if w > 2 else T
                if i == 0:
                    dve.wait_ge(kt_tr, 3 * h + 1)
                    dve.wait_ge(g_ready, h + 1)
                if i >= 2:
                    dve.wait_ge(lev_mm, 8 * h + i - 1)
                g, e = halves(G, w, n), halves(EX[i % 2], w, n)
                mid = g[:, :, 0, w - 1:w].to_broadcast([P, n // (2 * w), w])
                v.tensor_tensor(e[:, :, 0, :], mid, g[:, :, 0, :], ALU.subtract)
                v.tensor_tensor(e[:, :, 1, :], g[:, :, 1, :], mid, ALU.subtract).then_inc(diff_ready, 1)

            def decayed(h, i):
                w = LEVELS[i]
                n = SEQ if w > 2 else T
                e, q, k = halves(EX[i % 2], w, n), halves(Q, w, n), halves(K, w, n)
                dve.wait_ge(exp_ready, 11 * h + i + 1)
                v.tensor_tensor(e[:, :, 0, :], e[:, :, 0, :], k[:, :, 0, :], ALU.mult)
                v.tensor_tensor(e[:, :, 1, :], e[:, :, 1, :], q[:, :, 1, :], ALU.mult).then_inc(x_ready, 1)

            def take(h, i):
                dve.wait_ge(lev_mm, 8 * h + i + 1)
                dve.wait_ge(lev_read, 8 * h + i + 1)
                v.memset(pad[:, i:i + 1], 0.0)
                mask = (levmask[:, i, :] if i < 7 else ident[:]).bitcast(I32)
                for b in range(2):
                    last = v.copy_predicated(SC[:, 4 * b:4 * b + 4, :], mask[:, None, :].to_broadcast([P, 4, P]),
                                             banks[6 + b][:].rearrange("p (n t) -> p n t", n=4))
                if i >= 5:
                    last = v.copy_predicated(SC[0:NS, NP, 0:NS], mask[0:NS, 0:NS], banks[5][0:NS, 0:NS])
                last.then_inc(lev_read, 1)

            def turned(h, waited, to, ready):
                for b in range(2):
                    dve.wait_ge(waited, 3 * h + b + 2)
                    v.tensor_copy(to[:, 4 * b:4 * b + 4, :].rearrange("p n c -> p (n c)"), banks[3 + b][:]).then_inc(ready, 1)
                dve.wait_ge(waited, 3 * h + 4)
                v.tensor_copy(to[0:NS, NP, :], banks[5][0:NS, P:2 * P]).then_inc(ready, 1)

            with dve.Fori(0, HB) as h:
                dve.wait_ge(o_mm, h + 1)
                v.memset(SC[:], 0.0).then_inc(sc_zero, 1)
                dve.wait_ge(sig_ready, 2 * h + 1)
                v.tensor_scalar(K[:], K[:], lbw[:, bass.ds(h + 28, 1)], None, ALU.mult).then_inc(k_ready, 1)
                dve.wait_ge(f_ready, h + 1)
                v.tensor_tensor_scan(G[:], resets[:], EX[1][:], 0.0, ALU.mult, ALU.add).then_inc(g_ready, 1)
                dve.wait_ge(q_act, h + 1)
                dve.wait_ge(k_ready, h + 1)
                dve.wait_ge(sc_zero, h + 1)
                for i in range(9):
                    if i < 7:
                        diff(h, i)
                    if i == 1:
                        turned(h, vi_tr, VB, vb_ready)
                    if 1 <= i < 8:
                        decayed(h, i - 1)
                    if i >= 2:
                        take(h, i - 2)
                dve.wait_ge(lev_mm, 8 * h + 7)
                for a, b, w in ((0, SEQ, P), (SEQ, T, DQ)):
                    g = G[:, a:b].rearrange("p (n w) -> p n w", w=w)
                    last = v.tensor_tensor(EX[0][:, a:b].rearrange("p (n w) -> p n w", w=w),
                                           g[:, :, w - 1:w].to_broadcast([P, (b - a) // w, w]), g, ALU.subtract)
                last.then_inc(diff_ready, 1)
                dve.wait_ge(exp_ready, 11 * h + 8)
                v.tensor_tensor(EX[1][:], EX[1][:], Q[:], ALU.mult).then_inc(x_ready, 1)
                dve.wait_ge(exp_ready, 11 * h + 9)
                v.tensor_tensor(EX[0][:], EX[0][:], K[:], ALU.mult).then_inc(x_ready, 1)
                take(h, 7)
                turned(h, kt_tr, KT, kt_ready)
                for t in range(NP + 1):
                    rows = P if t < NP else NS
                    dve.wait_ge(v_tr, 3 * h + min(t // 4, 2) + 1)
                    src = banks[VBANK[t // 4]][0:rows, (t % 4) * P:(t % 4) * P + P] if t < NP else banks[5][0:NS, 0:P]
                    v.bn_stats(bst[0:rows, t, :], src).then_inc(v_own, 1)
                dve.wait_ge(v_own, 21 * h + 9)
                v.memset(pad[:, 8:9], 0.0)
                for t in range(NP + 1):
                    rows = P if t < NP else NS
                    last = v.bn_aggr(bmv[0:rows, t, :], bst[0:rows, t, :])
                last.then_inc(v_stat, 1)
                dve.wait_ge(kv_mm, h + 1)
                dve.wait_ge(exp_ready, 11 * h + 10)
                v.tensor_copy(SS[:, 0, :], banks[3][:, 0:P]).then_inc(st_chain, 1)
                for t in range(1, NP):
                    dve.wait_ge(st_chain, 8 * h + t)
                    v.scalar_tensor_tensor(out=SS[:, t, :], in0=SS[:, t - 1, :], scalar=DG[:, 0, t:t + 1],
                                           in1=banks[3 + t // 4][:, (t % 4) * P:(t % 4) * P + P],
                                           op0=ALU.mult, op1=ALU.add).then_inc(st_chain, 1)
                dve.wait_ge(v_std, h + 1)
                v.reciprocal(brs[:], brs[:]).then_inc(v_own, 1)
                dve.wait_ge(v_own, 21 * h + 10)
                for t in range(NP + 1):
                    rows = P if t < NP else NS
                    src = banks[VBANK[t // 4]][0:rows, (t % 4) * P:(t % 4) * P + P] if t < NP else banks[5][0:NS, 0:P]
                    v.tensor_scalar(VT[0:rows, t, :], src, bmv[0:rows, t, 0:1], brs[0:rows, t:t + 1],
                                    ALU.subtract, ALU.mult).then_inc(v_own, 1)
                dve.wait_ge(v_own, 21 * h + 19)
                for part, (r, a, b) in enumerate(((P, 0, NP), (NS, NP, NP + 1))):
                    x = VT[0:r, a:b, :]
                    v.tensor_tensor(x, x, gainA[0:r, bass.ds(h, 1), :].to_broadcast([r, b - a, P]), ALU.mult).then_inc(v_own, 1)
                for part, (r, a, b) in enumerate(((P, 0, NP), (NS, NP, NP + 1))):
                    dve.wait_ge(v_own, 21 * h + 20 + part)
                    x = VT[0:r, a:b, :]
                    v.tensor_tensor(x, x, biasA[0:r, bass.ds(h, 1), :].to_broadcast([r, b - a, P]), ALU.add).then_inc(vt_ready, 1)
                v.tensor_tensor(VX, VB[0:NS, NP:NP + 1, :].to_broadcast([NS, DEC, P]),
                                sel[:, :, None].to_broadcast([NS, DEC, P]), ALU.mult).then_inc(vx_ready, 1)
                dve.wait_ge(sv_mm, h + 1)
                dve.wait_ge(u_act, h + 1)
                for b, c, o in ((6, slice(0, 512), 0), (7, slice(512, SEQ), 0), (5, slice(SEQ, T), 256)):
                    n = c.stop - c.start
                    last = v.tensor_tensor(R[:, bass.ds(h, 1), c].rearrange("p k t -> p (k t)"), U[:, c],
                                           banks[b][:, o:o + n], ALU.mult)
                last.then_inc(a_done, 1)
                dve.wait_ge(o_mm, h + 2)
                dve.wait_ge(exp_ready, 11 * h + 11)
                v.tensor_tensor(S0[:], S0[:], DG[:, 1, :, None].to_broadcast([P, DEC, P]), ALU.mult).then_inc(sst_own, 1)
                dve.wait_ge(sst_own, 3 * h + 1)
                dve.wait_ge(skv_mm, h + 1)
                for b in range(2):
                    s4 = S0[:, 4 * b:4 * b + 4, :].rearrange("p n v -> p (n v)")
                    v.tensor_tensor(s4, s4, banks[3 + b][:], ALU.add).then_inc(sst_own, 1)
                dve.wait_ge(rms_std, 3 * h + 4)
                v.reciprocal(EX[0][:], EX[0][:]).then_inc(o_own, 1)
                dve.wait_ge(o_own, 2 * h + 1)
                v.scalar_tensor_tensor(out=K[:], in0=K[:], scalar=lbp[:, 12:13], in1=EX[0][:], op0=ALU.mult,
                                       op1=ALU.mult).then_inc(o_own, 1)
                dve.wait_ge(o_own, 2 * h + 2)
                dve.wait_ge(sg_act, h + 1)
                v.tensor_tensor(R[:, bass.ds(h + HB, 1), :].rearrange("p k t -> p (k t)"), K[:], SGG[:],
                                ALU.mult).then_inc(b_done, 1)

            for c in range(3):
                dve.wait_ge(m_hi, c + 1)
                v.tensor_tensor(HL[:, :, CH[c]], R[:, :, CH[c]], HH[:, :, CH[c]].bitcast(F32), ALU.subtract).then_inc(m_lo, 1)

            def attention_dve():
                dve.wait_ge(at_pool, 8)
                with dve.Fori(0, NPAIR) as hp:
                    def pages_copied(gs):
                        for g in gs:
                            dve.wait_ge(kp_tr, 16 * hp + g + 2)
                            if g >= 2:
                                dve.wait_ge(kp_z, 16 * hp + g - 1)
                            v.tensor_copy(KTP[g % 2][:], banks[3 + g % 2][:]).then_inc(kp_ev, 1)

                    for c in range(3):
                        dve.wait_ge(q_hi, 3 * hp + c + 1)
                        v.scalar_tensor_tensor(out=QL[:, CH[c]], in0=banks[c][:, 0:CW], scalar=0.125,
                                               in1=QH[:, CH[c]].bitcast(F32), op0=ALU.mult, op1=ALU.subtract).then_inc(qk_free, 1)
                    for c in range(3):
                        dve.wait_ge(k_hi, 3 * hp + c + 1)
                        v.tensor_tensor(KL[:, CH[c]], banks[c][:, 0:CW], KH[:, CH[c]].bitcast(F32), ALU.subtract).then_inc(qk_free, 1)
                        pages_copied(GROUPS_AT[c])
                    for c in range(3, 6):
                        if c == 3:
                            dve.wait_ge(kv_store, 64 * hp + 16)
                            for b in range(2):
                                dve.wait_ge(ktok_tr, 3 * hp + b + 1)
                                v.tensor_copy(KTOK[:, 4 * b:4 * b + 4, :].rearrange("p n c -> p (n c)"), banks[6 + b][:]).then_inc(ktok_ev, 1)
                        pages_copied(GROUPS_AT[c])

                    def sample_part(s):
                        if s == -2:
                            dve.wait_ge(ktok_tr, 3 * hp + 3)
                            v.tensor_copy(KTOK[0:NS, NP, :], banks[3][0:NS, 0:P]).then_inc(ktok_ev, 1)
                            dve.wait_ge(nz_ready, 2 * hp + 2)
                            v.tensor_tensor(NZ[:], NZ[:], capnew[:], ALU.min).then_inc(nz_own, 1)
                            dve.wait_ge(nz_own, hp + 1)
                            v.tensor_scalar(NE[:], NZ[:], ZCAP, None, ALU.min).then_inc(ne_min, 1)
                            dve.wait_ge(dz_ready, 2 * hp + 2)
                            v.tensor_scalar(DE[:], DZ[:], ZCAP, None, ALU.min).then_inc(de_min, 1)
                        if s == 0:
                            dve.wait_ge(ne_act, 2 * hp + 2)
                            v.tensor_tensor(NE[:], NE[:], NZ[:], ALU.max).then_inc(nsp_ready, 1)
                            v.memset(DSUF[:, :, PAGES - 1, :], 0.0).then_inc(dsuf, 1)
                        if s == 1:
                            dve.wait_ge(nsp_ready, hp + 1)
                            dve.wait_ge(dsuf, 9 * hp + 1)
                            v.tensor_copy(DSUF[0:NS, :, PAGES - 1, :], NE[:].rearrange("p n h i -> p n (h i)")).then_inc(dsuf, 1)
                            dve.wait_ge(de_act, 2 * hp + 2)
                            v.tensor_tensor(DE[:], DE[:], DZ[:], ALU.max).then_inc(dsp_ready, 1)
                        if s == 2:
                            dve.wait_ge(dsp_ready, hp + 1)
                        if 2 <= s <= 5:
                            for g in range(PAGES - 2 - 2 * (s - 2), max(PAGES - 4 - 2 * (s - 2), -1), -1):
                                dve.wait_ge(dsuf, 9 * hp + PAGES - g)
                                v.tensor_tensor(DSUF[:, :, g, :], DSUF[:, :, g + 1, :], DE[:, :, g + 1, :, :].rearrange("p n h i -> p n (h i)"),
                                                ALU.add).then_inc(dsuf, 1)
                        if s == 7:
                            dve.wait_ge(rn_mm, hp + 1)
                            v.tensor_tensor(NZ[:].rearrange("p n h i -> p (n h i)"), NZ[:].rearrange("p n h i -> p (n h i)"),
                                            banks[2][0:NS, 0:64], ALU.subtract).then_inc(narg, 1)
                            dve.wait_ge(rd_mm, hp + 1)
                            v.tensor_tensor(DZ[:].rearrange("p n g h i -> p (n g h i)"), DZ[:].rearrange("p n g h i -> p (n g h i)"),
                                            banks[5][:], ALU.subtract).then_inc(darg, 1)

                    def softplus_in(s):
                        c = slice(LOW[s], 512)
                        z, e = Z[s % 4], E[s % 2]
                        dve.wait_ge(zc, NST * hp + s + 1)
                        if DIAG[s]:
                            d = z[:, LOW[s]:LOW[s] + P]
                            v.tensor_tensor(d, d, cap[:], ALU.min).then_inc(capped, 1)
                            dve.wait_ge(capped, sum(DIAG) * hp + sum(DIAG[:s + 1]))
                        if s >= 2:
                            dve.wait_ge(spl_ready, NST * hp + s - 1)
                        v.tensor_scalar(e[:, c], z[:, c], ZCAP, None, ALU.min).then_inc(e_min, 1)

                    def softplus_out(s):
                        c = slice(LOW[s], 512)
                        dve.wait_ge(e_ln, NST * hp + s + 1)
                        v.tensor_tensor(E[s % 2][:, c], E[s % 2][:, c], Z[s % 4][:, c], ALU.max).then_inc(sp_ready, 1)
                        dve.wait_ge(sp_ready, NST * hp + s + 1)
                        if s >= 2:
                            if FINAL[s - 2]:
                                dve.wait_ge(tri_mm, NST * hp + s - 1)
                            else:
                                dve.wait_ge(carry_mm, NCARRY * hp + carries(s - 2))
                        v.tensor_copy(SPH[s % 2][:, c], E[s % 2][:, c]).then_inc(sph_ready, 1)

                    def exponent(s):
                        z = Z[s % 4][:, LOW[s]:512]
                        dve.wait_ge(tri_mm, NST * hp + s + 1)
                        v.tensor_tensor(z, z, banks[3][:, LOW[s]:512], ALU.subtract).then_inc(arg_ready, 1)

                    for s in range(-2, NST):
                        if s + 2 < NST:
                            softplus_in(s + 2)
                        if s == -2:
                            pages_copied(LATE_GROUPS)
                        if s >= 0:
                            exponent(s)
                        if s + 2 < NST:
                            softplus_out(s + 2)
                        sample_part(s)
                for c in range(3):
                    dve.wait_ge(m_hi, 3 + c + 1)
                    v.tensor_tensor(HL[:, :, CH[c]], R[:, :, CH[c]], HH[:, :, CH[c]].bitcast(F32), ALU.subtract).then_inc(m_lo, 1)

            def residual(stage, g, n=None):
                if n is not None:
                    dve.wait_ge(ln_mean, 3 * n)
                    v.memset(LSUM[:], 0.0).then_inc(ln_zero, 1)
                    dve.wait_ge(ln_zero, n + 1)
                with dve.Fori(0, KD // 2) as j:
                    for s in range(2):
                        for c in range(3):
                            u = 6 * j + 3 * s + c
                            r, xh, xl = (a[:, bass.ds(2 * j + s, 1), CH[c]].rearrange("p k t -> p (k t)") for a in (R, XH, XL))
                            dve.wait_ge(d_mm, 3 * TB[stage] + u + 5)
                            if g:
                                v.tensor_tensor(r, r, banks[c][:, 0:CW], ALU.add).then_inc(res1, 1)
                                if n is not None:
                                    dve.wait_ge(res1, units[stage] + u + 4)
                                    dve.wait_ge(ln_acc, 24 * n + u + 1)
                                    v.tensor_tensor(LSUM[:, CH[c]], LSUM[:, CH[c]], r, ALU.add).then_inc(ln_acc, 1)
                                continue
                            v.scalar_tensor_tensor(out=r, in0=xh.bitcast(F32), scalar=ALPHA, in1=banks[c][:, 0:CW],
                                                   op0=ALU.mult, op1=ALU.add).then_inc(res1, 1)
                            dve.wait_ge(res1, units[stage] + u + 4)
                            v.scalar_tensor_tensor(out=r, in0=xl.bitcast(F32), scalar=ALPHA, in1=r,
                                                   op0=ALU.mult, op1=ALU.add).then_inc(res, 1)
                            if n is not None:
                                dve.wait_ge(res, scaled[stage] + u + 1)
                                dve.wait_ge(ln_acc, 24 * n + u + 1)
                                v.tensor_tensor(LSUM[:, CH[c]], LSUM[:, CH[c]], r, ALU.add).then_inc(ln_acc, 1)

            def bcast(a, c):
                return a[:, None, CH[c]].to_broadcast([P, KD, CW])

            def norm_dve(n):
                dve.wait_ge(res1, ln_units[n][0] + 3)
                dve.wait_ge(res, ln_units[n][1])

                def centre(c):
                    dve.wait_ge(ln_mean, 3 * n + c + 1)
                    v.scalar_tensor_tensor(out=R[:, :, CH[c]], in0=banks[3 + c][:, None, 0:CW].to_broadcast([P, KD, CW]),
                                           scalar=-1.0 / D, in1=R[:, :, CH[c]], op0=ALU.mult, op1=ALU.add).then_inc(ln_cent, 1)

                def squares(c):
                    dve.wait_ge(ln_sq, 3 * n + c + 1)
                    v.tensor_reduce(LS[:, CH[c]], SQ[c % 2][:].rearrange("p k t -> p t k"), AX, ALU.add).then_inc(ln_sum2, 1)

                def scale(c):
                    dve.wait_ge(ln_std, 3 * n + c + 1)
                    v.reciprocal(RS[:, CH[c]], RS[:, CH[c]]).then_inc(ln_rstd, 1)
                    dve.wait_ge(ln_rstd, 3 * n + c + 1)
                    v.tensor_tensor(R[:, :, CH[c]], R[:, :, CH[c]], bcast(RS, c), ALU.mult).then_inc(ln_norm, 1)

                centre(0)
                centre(1)
                squares(0)
                centre(2)
                scale(0)
                squares(1)
                scale(1)
                squares(2)
                scale(2)
                if n < LAST_LN:
                    for c in (1, 2):
                        dve.wait_ge(x_hi, 3 * n + c + 1)
                        dve.wait_ge(x_lo, 3 * n + c)
                        v.tensor_tensor(XL[:, :, CH[c]], R[:, :, CH[c]], XH[:, :, CH[c]].bitcast(F32),
                                        ALU.subtract).then_inc(x_lo, 1)

            for l in range(LAYERS):
                if l == 1:
                    attention_dve()
                residual(("about", "cout")[l], 0, 2 * l)
                norm_dve(2 * l)
                for g, (_, kg) in enumerate(GROUPS):
                    done = ffn_pairs[l, g]
                    with dve.Fori(0, kg) as j:
                        for c in range(3):
                            dve.wait_ge(gate_read, 3 * done + 3 * j + c + 1)
                            dve.wait_ge(d_mm, 3 * TB["up", l, g] + 6 * j + 3 + c + 5)
                            dve.wait_ge(h_lo, 3 * done + 3 * j + c + 1)
                            v.tensor_tensor(HF[c][:], SG[c][:], banks[c][:, 0:CW], ALU.mult).then_inc(up_read, 1)
                        for c in range(3):
                            hh, hl = (a[:, bass.ds(j, 1), CH[c]].rearrange("p k t -> p (k t)") for a in (HH, HL))
                            dve.wait_ge(h_hi, 3 * done + 3 * j + c + 1)
                            v.tensor_tensor(hl, HF[c][:], hh.bitcast(F32), ALU.subtract).then_inc(h_lo, 1)
                    residual(("down", l, g), g, 2 * l + 1 if g == 2 else None)
                norm_dve(2 * l + 1)
            for n in range(NP + 1):
                rows = P if n < NP else NS
                for b in range(2):
                    dve.wait_ge(y_tr, 2 * n + b + 1)
                    if n >= 2:
                        dve.wait_ge(y_out[n % 2], 16 * (n // 2))
                    v.tensor_copy(YT[n % 2][0:rows, 512 * b:512 * b + 512], banks[2 * (n % 2) + b][0:rows, :]).then_inc(y_ev, 1)

        @block.tensor
        def _(pe):
            t = nc.tensor
            pe.wait_ge(set_pool, 7)
            pe.wait_ge(set_dve, 1)
            pe.wait_ge(par_load, 16 * 11)
            t.transpose(banks[6][:, 0:64], PROWS, ident[0:64, 0:64]).then_inc(par_mm, 1)
            t.transpose(banks[6][:, 64:77], LROWS, ident[0:13, 0:13]).then_inc(par_mm, 1)
            t.matmul(banks[6][:, 128:144], ones[0:1, :], BROW[:, 1024:1040], start=True, stop=True).then_inc(par_mm, 1)
            for h in range(HB):
                last = t.transpose(banks[7][:, h * P:(h + 1) * P], KT[:, h, :], ident[:])
            last.then_inc(par_mm, 2)
            for k in range(KD):
                if k >= 2:
                    pe.wait_ge(xt_lo, k - 1)
                if k == 0:
                    pe.wait_ge(x_load, 16 * (NP + 1))
                for n in range(NP):
                    t.transpose(banks[3 * (k % 2) + n // 4][:, (n % 4) * P:(n % 4) * P + P], XP[:, n, k * P:(k + 1) * P], ident[:])
                t.transpose(banks[3 * (k % 2) + 2][:, 0:NS], XS[:, k * P:(k + 1) * P], ident[0:NS, 0:NS]).then_inc(xt_mm, 1)
            pe.wait_ge(par_ev, 5)
            for i in range(2):
                t.matmul(banks[6 + i][:], ones[0:1, :], BROW[:, 512 * i:512 * i + 512], start=True, stop=True).then_inc(par_mm, 1)
            pe.wait_ge(xt_lo, KD)
            pe.wait_ge(par_ev, 8)
            pe.wait_ge(lb_own, 5)
            pe.wait_ge(ws_load, 16 * DEC)
            pe.wait_ge(wt_done, 1)

            def product(slot, kb, c, xh, xl):
                n = 0
                for k in range(kb):
                    for w, x in ((WH, xh), (WL, xh), (WH, xl)):
                        last = t.matmul(banks[c][:, 0:CW], w[slot][:, k, :], x[:, k, CH[c]],
                                        start=n == 0, stop=n == 3 * kb - 1)
                        n += 1
                return last.then_inc(d_mm, 1)

            def scores(h, i):
                if i < 7:
                    pe.wait_ge(x_ready, 9 * h + i + 1)
                pe.wait_ge(lev_read, 8 * h + i + 1)
                left, right = (K, Q) if i == 7 else (EX[i % 2], EX[i % 2])
                for n in range(NP):
                    c = slice(n * P, (n + 1) * P)
                    last = t.matmul(banks[6 + n // 4][:, (n % 4) * P:(n % 4) * P + P], left[:, c], right[:, c], start=True, stop=True)
                if i >= 5:
                    last = t.matmul(banks[5][0:NS, 0:NS], left[:, SEQ:T], right[:, SEQ:T], start=True, stop=True)
                last.then_inc(lev_mm, 1)

            def turn(src, b0, b2, o2, done):
                for n in range(NP):
                    last = t.transpose(banks[b0 + n // 4][:, (n % 4) * P:(n % 4) * P + P], src[:, n * P:(n + 1) * P], ident[:])
                    if n % 4 == 3:
                        last.then_inc(done, 1)
                t.transpose(banks[b2][0:NS, o2:o2 + P], src[:, SEQ:T], ident[:]).then_inc(done, 1)

            def q_units(h):
                for c in range(3):
                    if c == 0:
                        pe.wait_ge(w_split, 12 * h + 5)
                    pe.wait_ge(d_ev, 18 * h + c + 1)
                    product(0, KD, c, XH, XL)

            def head(h, last_head):
                n = 18 * h
                for j in range(1, 6):
                    for c in range(3):
                        if c == 0:
                            pe.wait_ge(w_split, 12 * h + 2 * j + 5)
                        pe.wait_ge(d_ev, n + 3 * j + c + 1)
                        product(j % 2, KD, c, XH, XL)
                        if 9 <= 3 * j + c < 17:
                            scores(h, 3 * j + c - 9)
                    if j == 2:
                        pe.wait_ge(d_ev, n + 12)
                        pe.wait_ge(rms_std, 3 * h + 1)
                        turn(U, 3, 5, P, vi_tr)
                pe.wait_ge(x_ready, 9 * h + 9)
                pe.wait_ge(vb_ready, 3 * h + 3)
                pe.wait_ge(lev_read, 8 * h + 9)
                turn(EX[0], 3, 5, P, kt_tr)
                pe.wait_ge(kt_ready, 3 * h + 3)
                pe.wait_ge(v_act, h + 1)
                turn(V, 6, 5, 0, v_tr)
                for m in range(NP):
                    last = t.matmul(banks[3 + m // 4][:, (m % 4) * P:(m % 4) * P + P], KT[:, m, :], VB[:, m, :], start=True, stop=True)
                last.then_inc(kv_mm, 1)
                if not last_head:
                    q_units(h + 1)
                pe.wait_ge(vt_ready, 2 * h + 2)
                for m in range(NP):
                    to = banks[6 + m // 4][:, (m % 4) * P:(m % 4) * P + P]
                    t.matmul(to, VT[:, m, :], WT[:, bass.ds(h, 1), :].rearrange("p h t -> p (h t)"), start=True, stop=False)
                    t.matmul(to, ones[0:1, :], bsrow[:, bass.ds(h, 1), :].rearrange("p h t -> p (h t)"), start=False, stop=True)
                to = banks[5][:, 256:256 + NS]
                t.matmul(to, VT[0:NS, NP, :], WS[:, bass.ds(h, 1), :].rearrange("p h t -> p (h t)"), start=True, stop=False)
                t.matmul(to, ones[0:1, :], bsS[:, bass.ds(h, 1), :, :].rearrange("p h n t -> p (h n t)"),
                         start=False, stop=True).then_inc(sv_mm, 1)
                pe.wait_ge(vx_ready, h + 1)
                pe.wait_ge(st_chain, 8 * h + 8)
                for b in range(2):
                    last = t.matmul(banks[3 + b][:], KT[0:NS, NP, :], VX[:, 4 * b:4 * b + 4, :].rearrange("p n v -> p (n v)"),
                                    start=True, stop=True)
                last.then_inc(skv_mm, 1)
                pe.wait_ge(a_done, h + 1)
                pe.wait_ge(s0_load, 16 * h + 16)
                for m in range(NP):
                    to = banks[6 + m // 4][:, (m % 4) * P:(m % 4) * P + P]
                    t.matmul(to, VB[:, m, :], SC[:, m, :], start=True, stop=m == 0)
                    if m:
                        t.matmul(to, SS[:, m - 1, :], EX[1][:, m * P:(m + 1) * P], start=False, stop=True)
                t.matmul(banks[5][:, 0:NS], VB[0:NS, NP, :], SC[0:NS, NP, 0:NS], start=True, stop=False, skip_group_check=True)
                for m in range(DEC):
                    last = t.matmul(banks[5][:, DQ * m:DQ * m + DQ], S0[:, m, :], EX[1][:, SEQ + DQ * m:SEQ + DQ * m + DQ],
                                    start=False, stop=True, skip_group_check=True)
                last.then_inc(o_mm, 1)
                pe.wait_ge(osq, h + 1)
                pe.wait_ge(sst_own, 3 * h + 3)
                for c in range(3):
                    last = t.matmul(banks[3 + c][:, 0:CW], ones[:], G[:, CH[c]], start=True, stop=True)
                last.then_inc(ms_mm, 1)

            q_units(0)
            with pe.Fori(0, HB - 1) as h:
                head(h, False)
            head(HB - 1, True)

            def attention_pe():
                n0 = TB["c"]
                pe.wait_ge(res1, units["down", 0, 2] + 3 * KD + 3)
                pe.wait_ge(ln_std, 6)
                pe.wait_ge(ln_cent, 6)
                pe.wait_ge(at_pool, 8)
                def q_products(hp, first, count):
                    for i in range(first, first + count):
                        c, m = divmod(i, 3 * KD)
                        k, part = divmod(m, 3)
                        if i == 0:
                            pe.wait_ge(w_split, 2 * (n0 + 3 * hp) + 5)
                        if i == 6 * KD:
                            pe.wait_ge(narg, hp + 1)
                        if m == 0:
                            pe.wait_ge(v_free, 3 * hp + c + 1)
                        w, x = ((WH, XH), (WL, XH), (WH, XL))[part]
                        last = t.matmul(banks[c][:, 0:CW], w[0][:, k, :], x[:, k, CH[c]], start=m == 0, stop=m == 3 * KD - 1,
                                        skip_group_check=True)
                        if m == 3 * KD - 1:
                            last.then_inc(d_mm, 1)

                def pair(hp, last_pair):
                    n = n0 + 3 * hp

                    def turn_pages(g):
                        if g % 2 == 0:
                            pe.wait_ge(pg_load[g // 2 % 4], 16 * PAGES * (4 * hp + g // 8 + 1))
                        if g >= 2:
                            pe.wait_ge(kp_ev, 16 * hp + g - 1)
                        for i in range(4):
                            last = t.transpose(banks[3 + g % 2][:, i * P:(i + 1) * P], PG[g // 2 % 4][:, 4 * (g % 2) + i, :], ident[:])
                        last.then_inc(kp_tr, 1)

                    def page_logits(g):
                        pe.wait_ge(kp_ev, 16 * hp + g + 1)
                        if g == 0:
                            pe.wait_ge(q_hi, 3 * hp + 3)
                            pe.wait_ge(do_ev, 2 * hp + 1)
                        for i in range(4):
                            o = 64 * (g // 2) + 8 * (4 * (g % 2) + i)
                            last = t.matmul(banks[5][:, o:o + 8], KTP[g % 2][:, i * P:(i + 1) * P],
                                            QD[:, g // 2].rearrange("p h i -> p (h i)"), start=True, stop=True)
                        last.then_inc(kp_z, 1)

                    def turn_tokens(src, bs, done):
                        for m in range(NP):
                            last = t.transpose(banks[bs[m // 4]][:, (m % 4) * P:(m % 4) * P + P], src[:, m * P:(m + 1) * P], ident[:])
                            if m % 4 == 3:
                                last.then_inc(done, 1)

                    def logits(s):
                        h, c, b = STEPS[s]
                        r, lo = slice(64 * h, 64 * h + 64), LOW[s]
                        if s < 2:
                            pe.wait_ge(qk_free, 6 * hp + 6)
                        else:
                            pe.wait_ge(zc, NST * hp + s - 1)
                        for i, (k, q) in enumerate(((KH, QH), (KL, QH), (KH, QL))):
                            last = t.matmul(banks[6 + s % 2][:, lo:512], k[r, b * P:(b + 1) * P], q[r, 512 * c + lo:512 * c + 512],
                                            start=i == 0, stop=i == 2)
                        last.then_inc(z_mm, 1)

                    def sums(s, m, first, done):
                        lo = LOW[s]
                        t.matmul(banks[3][:, lo:512], m[:], SPH[s % 2][:, lo:512], start=first, stop=False, skip_group_check=True)
                        t.matmul(banks[3][:, lo:512], m[:], SPL[s % 2][:, lo:512], start=False, stop=True,
                                 skip_group_check=True).then_inc(done, 1)

                    def values(s):
                        h, c, b = STEPS[s]
                        r, lo = slice(64 * h, 64 * h + 64), LOW[s]
                        pe.wait_ge(w_ready, NST * hp + s + 1)
                        if FIRST[s]:
                            pe.wait_ge(po_ev, 4 * hp + chunks_done(s) + 1)
                            pe.wait_ge(nz_ready, 2 * hp + 2)
                        t.matmul(banks[4][r, lo:512], VTOK[:, b, r], Z[s % 4][:, lo:512], start=FIRST[s], stop=FINAL[s],
                                 skip_group_check=True).then_inc(pv_mm, 1)

                    def sample_values(m):
                        if m == 0:
                            pe.wait_ge(dw_ready, hp + 1)
                            pe.wait_ge(nw_ready, hp + 1)
                        pe.wait_ge(pg_load[m % 4], 16 * PAGES * (4 * hp + m // 4 + 3))
                        to = banks[5][:, 8 * m:8 * m + 8]
                        for g in range(PAGES):
                            t.matmul(to, PG[m % 4][:, g, :], DE[:, m, g].rearrange("p h i -> p (h i)"), start=g == 0, stop=False)
                        t.matmul(to, VTOK[0:NS, NP, :], NE[:, m].rearrange("p h i -> p (h i)"), start=False, stop=True).then_inc(dv_mm, 1)

                    for j in (1, 2):
                        for c in range(3):
                            if c == 0:
                                pe.wait_ge(w_split, 2 * n + 2 * j + 5)
                            pe.wait_ge(qk_free, 6 * hp + 3 * (j - 1) + c + 1)
                            product(j % 2, KD, c, XH, XL)
                            if j == 1 and c == 0:
                                pe.wait_ge(po_ev, 4 * hp + 1)
                            if j == 2 and c == 0:
                                pe.wait_ge(k_hi, 3 * hp + 3)
                                turn_tokens(KF, (6, 7), ktok_tr)
                            for g in GROUPS_AT[3 * (j - 1) + c]:
                                turn_pages(g)
                                if g:
                                    page_logits(g - 1)
                    for s in range(2):
                        pe.wait_ge(ktok_ev, 3 * hp + s + 1)
                        logits(s)
                    for g in LATE_GROUPS:
                        turn_pages(g)
                        page_logits(g - 1)
                    page_logits(15)
                    t.transpose(banks[3][0:NS, 0:P], KF[:, SEQ:T], ident[:]).then_inc(ktok_tr, 1)
                    t.matmul(banks[4][0:NS, 0:64], KF[:, SEQ:T], QD[:].rearrange("p n h i -> p (n h i)"), start=True, stop=True).then_inc(zn_mm, 1)
                    pe.wait_ge(v_free, 3 * hp + 6)
                    turn_tokens(VI, (0, 1), vtok_tr)
                    t.transpose(banks[2][0:NS, 0:P], VI[:, SEQ:T], ident[:]).then_inc(vtok_tr, 1)
                    logits(2)
                    pe.wait_ge(ktok_ev, 3 * hp + 3)
                    pe.wait_ge(vtok_ev, 3 * hp + 3)
                    for s in range(NST):
                        pe.wait_ge(spl_ready, NST * hp + s + 1)
                        if FIRST[s] and s:
                            pe.wait_ge(arg_ready, NST * hp + s)
                        sums(s, triR, FIRST[s], tri_mm)
                        if s:
                            values(s - 1)
                        if s + 3 < NST:
                            logits(s + 3)
                        if s == 6:
                            pe.wait_ge(nsp_ready, hp + 1)
                            t.matmul(banks[2][:, 0:64], tri[0:NS, :], NE[:].rearrange("p n h i -> p (n h i)"), start=True,
                                     stop=True).then_inc(rn_mm, 1)
                            pe.wait_ge(dsuf, 9 * hp + 9)
                            pe.wait_ge(dz_ready, 2 * hp + 2)
                            t.matmul(banks[5][:], tri[:], DE[:].rearrange("p n g h i -> p (n g h i)"), start=True, stop=False)
                            t.matmul(banks[5][:], ones[:], DSUF[:].rearrange("p n g i -> p (n g i)"), start=False, stop=True).then_inc(rd_mm, 1)
                        if s >= 9 and s % 2:
                            sample_values((s - 9) // 2)
                        if s >= Q_FIRST and s % 2 == 0 and not last_pair:
                            q_products(hp + 1, Q_COUNT * ((s - Q_FIRST) // 2), Q_COUNT)
                        if not FINAL[s]:
                            pe.wait_ge(arg_ready, NST * hp + s + 1)
                            sums(s, restR, False, carry_mm)
                    values(NST - 1)

                for c in range(3):
                    pe.wait_ge(x_lo, 3 + c + 1)
                    q_products(0, 3 * KD * c, 3 * KD)
                with pe.Fori(0, NPAIR - 1) as hp:
                    pair(hp, False)
                pair(NPAIR - 1, True)

            def out_stage(stage, kb, mixed=None):
                with pe.Fori(0, KD // 2) as j:
                    for s in range(2):
                        for c in range(3):
                            if c == 0:
                                pe.wait_ge(w_split, 2 * TB[stage] + 4 * j + 2 * s + 5)
                            if mixed is not None:
                                pe.wait_ge(m_lo, 3 * mixed + c + 1)
                            pe.wait_ge(res1, units[stage] + 6 * j + 3 * s + c + 1)
                            product(s, kb, c, HH, HL)

            def norm_pe(n):
                for c in range(3):
                    pe.wait_ge(ln_acc, 24 * n + 25 + c)
                    t.matmul(banks[3 + c][:, 0:CW], ones[:], LSUM[:, CH[c]], start=True, stop=True).then_inc(ln_mean, 1)
                for c in range(3):
                    pe.wait_ge(ln_sum2, 3 * n + c + 1)
                    if c == 2:
                        pe.wait_ge(ln_cent, 3 * n + 1)
                    t.matmul(banks[VARB[c]][:, 0:CW], ones[:], LS[:, CH[c]], start=True, stop=True).then_inc(ln_var, 1)

            for l in range(LAYERS):
                if l == 1:
                    attention_pe()
                out_stage(("about", "cout")[l], KD, l)
                norm_pe(2 * l)
                for g, (_, kg) in enumerate(GROUPS):
                    stage, done = ("up", l, g), ffn_pairs[l, g]
                    if g:
                        pe.wait_ge(res1, units["down", l, g - 1] + 3 * KD + 3)
                    with pe.Fori(0, kg) as j:
                        for s in range(2):
                            for c in range(3):
                                if c == 0:
                                    pe.wait_ge(w_split, 2 * TB[stage] + 4 * j + 2 * s + 5)
                                if s == 0:
                                    pe.wait_ge(x_lo, 6 * l + c + 1)
                                    pe.wait_ge(up_read, 3 * done + 3 * j + c + 1)
                                else:
                                    pe.wait_ge(gate_read, 3 * done + 3 * j + c + 1)
                                product(s, KD, c, XH, XL)
                    pe.wait_ge(h_lo, 3 * (done + kg) + 3)
                    out_stage(("down", l, g), kg)
                norm_pe(2 * l + 1)
            for n in range(NP + 1):
                rows = P if n < NP else NS
                pe.wait_ge(ln_aff, 24 * LAST_LN + 8 * ((n * P + rows - 1) // CW + 1))
                if n == 1:
                    pe.wait_ge(ln_std, 3 * LAST_LN + 3)
                if n >= 2:
                    pe.wait_ge(y_ev, 2 * n - 2)
                for k in range(KD):
                    last = t.transpose(banks[2 * (n % 2) + k // 4][0:rows, (k % 4) * P:(k % 4) * P + P],
                                       R[:, k, n * P:n * P + rows], ident[:])
                    if k % 4 == 3:
                        last.then_inc(y_tr, 1)


_INS = ["x_prompt", "x_sample", "state_b", "cache_k", "cache_v", "page_table", "ab_w_in", "ab_w_out", "a_w_s",
        "a_b_s", "a_ln_g", "a_ln_b", "b_lb_logits", "b_norm_g", "c_w_in", "c_w_out", "c_logit_bias", "ln1_g",
        "ln1_b", "ln2_g", "ln2_b", "ffn_w_gate", "ffn_w_up", "ffn_w_down"]
_OUTS = [(1, SEQ, D), (DEC, DQ, D), (1, DEC, DQ, 512), (1, 1, HB, P, P), (1, DEC, HB, P, P),
         (1, 1, SEQ, 16, 64), (1, 1, SEQ, 16, 64), (1, DEC, DQ, 16, 64), (1, DEC, DQ, 16, 64)]


def kernel(**inputs):
    import numpy as _np
    import concourse.bacc as _bacc
    from concourse import mybir as _mybir
    from concourse.bass_utils import run_bass_kernel_spmd as _run

    nc = _bacc.Bacc("TRN2", target_bir_lowering=False, num_devices=1)
    arrays, args = {}, []
    for name in _INS:
        a = _np.ascontiguousarray(inputs[name])
        arrays[f"in_{name}_dram"] = a
        args.append(nc.dram_tensor(f"in_{name}_dram", a.shape, _mybir.dt.from_np(a.dtype), kind="ExternalInput").ap())
    for i, shape in enumerate(_OUTS):
        args.append(nc.dram_tensor(f"out_{i}_dram", shape, _mybir.dt.float32, kind="ExternalOutput").ap())
    hybrid_step(nc, *args)
    r = _run(nc, [arrays], core_ids=[0])
    return tuple(r.results[0][f"out_{i}_dram"] for i in range(len(_OUTS)))
```
